# Optimizing a Trainium2 kernel written in Bass

```python
import jax, jax.numpy as jnp
from jax import lax
import numpy as np

D_MODEL = 1024
BATCH = 1
SEQ = 512
DEPTH = 2

N_MIXERS = 2
EXPAND = 2
D_INNER = EXPAND * D_MODEL
CONV_WIDTH = 31
CONV_IN_PROJ = 3 * D_INNER
RET_HEADS = 4
RET_QK_DIM = D_MODEL // RET_HEADS
RET_V_DIM = D_INNER // RET_HEADS
RET_IN_PROJ = 2 * RET_HEADS * RET_QK_DIM + 2 * D_INNER
CHUNK = 128
ROPE_BASE = 10000.0
EPS = 1e-6
N_CONV_LAYERS = (DEPTH + 1) // 2
N_RET_LAYERS = DEPTH // 2


def rms_norm(x, g):
    xf = x.astype(jnp.float32)
    y = xf * lax.rsqrt(jnp.mean(xf * xf, axis=-1, keepdims=True) + EPS)
    return (y * g.astype(jnp.float32)).astype(x.dtype)

def conv_module(h, w_in, dw_w, dw_b, ln_g, ln_b, w_out):
    proj = h @ w_in
    a, b, z = jnp.split(proj, 3, axis=-1)
    u = a * jax.nn.sigmoid(b)
    c = lax.conv_general_dilated(
        u, dw_w[:, None, :].astype(u.dtype), window_strides=(1,),
        padding=((CONV_WIDTH - 1, 0),),
        dimension_numbers=("NWC", "WIO", "NWC"),
        feature_group_count=D_INNER) + dw_b
    cf = c.astype(jnp.float32)
    mu = jnp.mean(cf, axis=-1, keepdims=True)
    var = jnp.mean(jnp.square(cf - mu), axis=-1, keepdims=True)
    cn = ((cf - mu) * lax.rsqrt(var + EPS) * ln_g.astype(jnp.float32) + ln_b.astype(jnp.float32))
    y = jax.nn.silu(cn).astype(h.dtype) * jax.nn.silu(z)
    return y @ w_out

def apply_rotary(t, cos, sin):
    t1, t2 = jnp.split(t.astype(jnp.float32), 2, axis=-1)
    return jnp.concatenate([t1 * cos - t2 * sin, t1 * sin + t2 * cos], axis=-1).astype(t.dtype)

def retention_module(h, positions, w_in, w_out):
    bsz, seq, _ = h.shape
    nc = seq // CHUNK
    qk_w = RET_HEADS * RET_QK_DIM
    proj = h @ w_in
    q, k, v, g = jnp.split(proj, [qk_w, 2 * qk_w, 2 * qk_w + D_INNER], axis=-1)
    q = q.reshape(bsz, seq, RET_HEADS, RET_QK_DIM)
    k = k.reshape(bsz, seq, RET_HEADS, RET_QK_DIM)
    v = v.reshape(bsz, seq, RET_HEADS, RET_V_DIM)

    inv_freq = ROPE_BASE ** (-jnp.arange(RET_QK_DIM // 2, dtype=jnp.float32) / (RET_QK_DIM // 2))
    ang = positions.astype(jnp.float32)[..., None] * inv_freq
    cos, sin = jnp.cos(ang)[:, :, None, :], jnp.sin(ang)[:, :, None, :]
    q = apply_rotary(q, cos, sin)
    k = apply_rotary(k, cos, sin) * (RET_QK_DIM ** -0.5)

    qc = q.reshape(bsz, nc, CHUNK, RET_HEADS, RET_QK_DIM)
    kc = k.reshape(bsz, nc, CHUNK, RET_HEADS, RET_QK_DIM)
    vc = v.reshape(bsz, nc, CHUNK, RET_HEADS, RET_V_DIM)

    log_gamma = jnp.log(1.0 - 2.0 ** (-5.0 - jnp.arange(RET_HEADS, dtype=jnp.float32)))
    idx = jnp.arange(CHUNK, dtype=jnp.float32)
    diff = idx[:, None] - idx[None, :]
    causal = diff >= 0
    inner_decay = jnp.where(causal[None], jnp.exp(jnp.where(causal, diff, 0.0)[None] * log_gamma[:, None, None]), 0.0)
    q_decay = jnp.exp((idx + 1.0)[:, None] * log_gamma)[..., None]
    k_decay = jnp.exp((CHUNK - 1.0 - idx)[:, None] * log_gamma)[..., None]
    chunk_decay = jnp.exp(CHUNK * log_gamma)[:, None, None]

    scores = jnp.einsum("bnihd,bnjhd->bnhij", qc, kc) * inner_decay
    inner = jnp.einsum("bnhij,bnjhe->bnihe", scores, vc)

    def step(state, xs):
        qn, kn, vn = xs
        cross = jnp.einsum("bihd,bhde->bihe", qn * q_decay, state)
        state = state * chunk_decay + jnp.einsum("bjhd,bjhe->bhde", kn * k_decay, vn)
        return state, cross

    state0 = jnp.zeros((bsz, RET_HEADS, RET_QK_DIM, RET_V_DIM), jnp.float32)
    _, cross = lax.scan(step, state0, (jnp.moveaxis(qc, 1, 0), jnp.moveaxis(kc, 1, 0), jnp.moveaxis(vc, 1, 0)))
    o = (inner + jnp.moveaxis(cross, 0, 1)).astype(jnp.float32).reshape(bsz, seq, RET_HEADS, RET_V_DIM)

    o = o * lax.rsqrt(jnp.mean(o * o, axis=-1, keepdims=True) + EPS)
    o = o.reshape(bsz, seq, D_INNER).astype(h.dtype)
    return (jax.nn.silu(g) * o) @ w_out

def first_inputs(seed: int = 0) -> dict:
    key = jax.random.key(seed)
    ks = jax.random.split(key, 14)
    f32 = jnp.float32
    x = jax.random.normal(ks[0], (BATCH, SEQ, D_MODEL), f32)
    positions = jnp.broadcast_to(jnp.arange(SEQ, dtype=jnp.int32), (BATCH, SEQ))
    conv_norm = 1.0 + 0.01 * jax.random.normal(ks[1], (N_CONV_LAYERS, D_MODEL), f32)
    conv_w_in = jax.random.normal(ks[2], (N_CONV_LAYERS, D_MODEL, CONV_IN_PROJ), f32) * D_MODEL ** -0.5
    conv_dw_w = jax.random.normal(ks[3], (N_CONV_LAYERS, CONV_WIDTH, D_INNER), f32) * CONV_WIDTH ** -0.5
    conv_dw_b = 0.01 * jax.random.normal(ks[4], (N_CONV_LAYERS, D_INNER), f32)
    conv_ln_g = 1.0 + 0.01 * jax.random.normal(ks[5], (N_CONV_LAYERS, D_INNER), f32)
    conv_ln_b = 0.01 * jax.random.normal(ks[6], (N_CONV_LAYERS, D_INNER), f32)
    conv_w_out = jax.random.normal(ks[7], (N_CONV_LAYERS, D_INNER, D_MODEL), f32) * (0.5 * D_INNER ** -0.5)
    ret_norm = 1.0 + 0.01 * jax.random.normal(ks[8], (N_RET_LAYERS, D_MODEL), f32)
    ret_w_in = jax.random.normal(ks[9], (N_RET_LAYERS, D_MODEL, RET_IN_PROJ), f32) * D_MODEL ** -0.5
    ret_w_out = jax.random.normal(ks[10], (N_RET_LAYERS, D_INNER, D_MODEL), f32) * (0.5 * D_INNER ** -0.5)
    final_norm = 1.0 + 0.01 * jax.random.normal(ks[11], (D_MODEL,), f32)
    return {"x": x, "positions": positions,
            "conv_norm": conv_norm, "conv_w_in": conv_w_in, "conv_dw_w": conv_dw_w, "conv_dw_b": conv_dw_b,
            "conv_ln_g": conv_ln_g, "conv_ln_b": conv_ln_b, "conv_w_out": conv_w_out,
            "ret_norm": ret_norm, "ret_w_in": ret_w_in, "ret_w_out": ret_w_out,
            "final_norm": final_norm}

def first_block(x, positions, conv_norm, conv_w_in, conv_dw_w, conv_dw_b, conv_ln_g, conv_ln_b, conv_w_out,
              ret_norm, ret_w_in, ret_w_out, final_norm):
    for i in range(DEPTH):
        j = i // N_MIXERS
        if i % N_MIXERS == 0:
            h = rms_norm(x, conv_norm[j])
            y = conv_module(h, conv_w_in[j], conv_dw_w[j], conv_dw_b[j], conv_ln_g[j], conv_ln_b[j], conv_w_out[j])
        else:
            h = rms_norm(x, ret_norm[j])
            y = retention_module(h, positions, ret_w_in[j], ret_w_out[j])
        x = x + y.astype(x.dtype)
    return rms_norm(x, final_norm)


_first_inputs = first_inputs


def first_inputs(seed=0):
    import zlib

    import numpy as np

    out = dict(_first_inputs(seed))
    spreads = {}
    factors = {'conv_norm': 22.618,
     'conv_dw_b': 79.809,
     'conv_ln_g': 200.0,
     'conv_ln_b': 200.0,
     'ret_norm': 200.0,
     'final_norm': 181.536}
    for name, (base, spread) in spreads.items():
        noise = np.random.default_rng([zlib.crc32(name.encode()), seed]).standard_normal(out[name].shape)
        drawn = base * np.exp(spread * noise) if base else spread * noise
        out[name] = __import__('jax').numpy.asarray(drawn.astype(out[name].dtype))
    for name, factor in factors.items():
        out[name] = (out[name] * factor).astype(out[name].dtype)
    return out


_narrow_inputs = first_inputs


def first_inputs(seed=0):

    out = dict(_narrow_inputs(seed))
    wider = {'conv_ln_g': 6.16, 'conv_ln_b': 6.22, 'ret_norm': 12.0, 'final_norm': 6.38}
    for name, times in wider.items():
        mean = out[name].mean()
        out[name] = (mean + times * (out[name] - mean)).astype(out[name].dtype)
    return out


CTX_LEN = 256
GRID_W = 64
HEAD_DIM = 64
N_HEADS = 8
N_KV_HEADS = 2
GQA = N_HEADS // N_KV_HEADS
ATTN_WIDTH = N_HEADS * HEAD_DIM
KV_WIDTH = N_KV_HEADS * HEAD_DIM
WINDOW = 128
ATTN_BLOCK = 128
ATTN_SCALE = HEAD_DIM ** -0.5
CONV_WIDTH_2 = D_MODEL // 4
GM_WIDTH = D_MODEL // 4
GM_GROUPS = 4
GM_HEAD = GM_WIDTH // GM_GROUPS
MIX_WIDTH = ATTN_WIDTH + CONV_WIDTH_2 + GM_WIDTH
IN_WIDTH = ATTN_WIDTH + 2 * KV_WIDTH + 3 * CONV_WIDTH_2 + 2 * GM_WIDTH
SPLIT_POINTS = (ATTN_WIDTH,
                ATTN_WIDTH + KV_WIDTH,
                ATTN_WIDTH + 2 * KV_WIDTH,
                ATTN_WIDTH + 2 * KV_WIDTH + CONV_WIDTH_2,
                ATTN_WIDTH + 2 * KV_WIDTH + 2 * CONV_WIDTH_2,
                ATTN_WIDTH + 2 * KV_WIDTH + 3 * CONV_WIDTH_2,
                ATTN_WIDTH + 2 * KV_WIDTH + 3 * CONV_WIDTH_2 + GM_WIDTH)
N_GROUPS = 4
EXP_PER_GROUP = 8
N_EXPERTS = N_GROUPS * EXP_PER_GROUP
TOP_K = 2
D_EXPERT = D_MODEL // 2
MOE_BLOCK = 128
ALPHA = (2 * DEPTH) ** 0.25
BETA = (8 * DEPTH) ** -0.25
LN_EPS = 1e-6
NEG_INF = -1e30


def layer_norm(x, g=None, b=None):
    xf = x.astype(jnp.float32)
    mu = jnp.mean(xf, axis=-1, keepdims=True)
    var = jnp.mean(jnp.square(xf - mu), axis=-1, keepdims=True)
    y = (xf - mu) * lax.rsqrt(var + LN_EPS)
    if g is not None:
        y = y * g.astype(jnp.float32) + b.astype(jnp.float32)
    return y.astype(x.dtype)

def _rope(x, pos):
    m = x.shape[-1] // 2
    freqs = ROPE_BASE ** (-jnp.arange(m, dtype=jnp.float32) / m)
    ang = pos.astype(jnp.float32)[:, None] * freqs[None, :]
    cos = jnp.cos(ang)[None, :, None, :]
    sin = jnp.sin(ang)[None, :, None, :]
    xf = x.astype(jnp.float32)
    a, b = xf[..., :m], xf[..., m:]
    return jnp.concatenate([a * cos - b * sin, b * cos + a * sin], axis=-1).astype(x.dtype)

def axial_rope(x, row, col):
    half = x.shape[-1] // 2
    return jnp.concatenate([_rope(x[..., :half], row), _rope(x[..., half:], col)], axis=-1)

def short_conv(u, w):
    up = jnp.pad(u, ((0, 0), (1, 1), (0, 0)))
    return up[:, :-2] * w[0] + up[:, 1:-1] * w[1] + up[:, 2:] * w[2]

def local_mixers(cb, cc, cx, gu, gv, conv_w, gm_ws, gm_bs):
    y_conv = cb * short_conv(cc * cx, conv_w)
    b_, l_ = gu.shape[:2]
    u = jax.nn.gelu(gu)
    v = layer_norm(jax.nn.gelu(gv)).reshape(b_, l_ // CHUNK, CHUNK, GM_GROUPS, GM_HEAD)
    s = jnp.einsum('gpq,bnqgc->bnpgc', gm_ws, v) + gm_bs.T[None, None, :, :, None]
    y_gm = u * s.reshape(b_, l_, GM_WIDTH).astype(u.dtype)
    return jnp.concatenate([y_conv, y_gm], axis=-1)

def sink_softmax(s, sink):
    col = jnp.broadcast_to(sink.astype(jnp.float32).reshape(N_KV_HEADS, GQA)[None, :, :, None, None],
                           s.shape[:-1] + (1,))
    return jax.nn.softmax(jnp.concatenate([col, s], axis=-1), axis=-1)[..., 1:]

def window_attention(q, k, v, k_ctx, v_ctx, sink):
    b_, s_ = q.shape[:2]
    nb = s_ // ATTN_BLOCK
    pad = ((0, 0), (ATTN_BLOCK, ATTN_BLOCK), (0, 0), (0, 0))
    kp, vp = jnp.pad(k, pad), jnp.pad(v, pad)
    span = 3 * ATTN_BLOCK
    rel = (jnp.arange(span)[None, :] - ATTN_BLOCK) - jnp.arange(ATTN_BLOCK)[:, None]
    band = jnp.abs(rel) <= WINDOW

    def one_block(n):
        start = n * ATTN_BLOCK
        qn = lax.dynamic_slice_in_dim(q, start, ATTN_BLOCK, axis=1).reshape(
            b_, ATTN_BLOCK, N_KV_HEADS, GQA, HEAD_DIM)
        kn = lax.dynamic_slice_in_dim(kp, start, span, axis=1)
        vn = lax.dynamic_slice_in_dim(vp, start, span, axis=1)
        kpos = start - ATTN_BLOCK + jnp.arange(span)
        valid = band & ((kpos >= 0) & (kpos < s_))[None, :]
        s_loc = jnp.einsum('bqkgd,bskd->bkgqs', qn, kn, preferred_element_type=jnp.float32) * ATTN_SCALE
        s_loc = jnp.where(valid, s_loc, NEG_INF)
        s_ctx = jnp.einsum('bqkgd,bckd->bkgqc', qn, k_ctx, preferred_element_type=jnp.float32) * ATTN_SCALE
        p = sink_softmax(jnp.concatenate([s_loc, s_ctx], axis=-1), sink).astype(v.dtype)
        o = (jnp.einsum('bkgqs,bskd->bqkgd', p[..., :span], vn)
             + jnp.einsum('bkgqc,bckd->bqkgd', p[..., span:], v_ctx))
        return o.reshape(b_, ATTN_BLOCK, ATTN_WIDTH)

    out = lax.map(one_block, jnp.arange(nb))
    return out.transpose(1, 0, 2, 3).reshape(b_, s_, ATTN_WIDTH)

def context_attention(q, k, v, sink):
    b_, c_ = q.shape[:2]
    qg = q.reshape(b_, c_, N_KV_HEADS, GQA, HEAD_DIM)
    s = jnp.einsum('bqkgd,bckd->bkgqc', qg, k, preferred_element_type=jnp.float32) * ATTN_SCALE
    p = sink_softmax(s, sink).astype(v.dtype)
    o = jnp.einsum('bkgqc,bckd->bqkgd', p, v)
    return o.reshape(b_, c_, ATTN_WIDTH)

def hier_moe(h, w_rg, b_rg, w_re, b_re, w1, w3, w2):
    n, d_ = h.shape
    hf = h.astype(jnp.float32)
    g_logit = hf @ w_rg.astype(jnp.float32) + b_rg.astype(jnp.float32)
    g_val, g_idx = lax.top_k(g_logit, 1)
    p_group = jnp.exp(g_val[:, 0] - jax.nn.logsumexp(g_logit, axis=-1))
    e_logit = (hf @ w_re.astype(jnp.float32)).reshape(n, N_GROUPS, EXP_PER_GROUP) \
        + b_re.astype(jnp.float32).reshape(N_GROUPS, EXP_PER_GROUP)
    e_logit = jnp.take_along_axis(e_logit, g_idx[:, :, None], axis=1)[:, 0]
    e_val, e_idx = lax.top_k(e_logit, TOP_K)
    gates = p_group[:, None] * jax.nn.softmax(e_val, axis=-1)
    expert = g_idx * EXP_PER_GROUP + e_idx

    a = n * TOP_K
    flat_e = expert.reshape(-1)
    flat_g = gates.reshape(-1)
    order = jnp.argsort(flat_e)
    se = flat_e[order]
    counts = jnp.bincount(flat_e, length=N_EXPERTS)
    starts = jnp.cumsum(counts) - counts
    padded = (counts + MOE_BLOCK - 1) // MOE_BLOCK * MOE_BLOCK
    pends = jnp.cumsum(padded)
    pstarts = pends - padded
    dest = pstarts[se] + jnp.arange(a) - starts[se]
    n_blocks = -(-a // MOE_BLOCK) + N_EXPERTS
    slot_tok = jnp.zeros(n_blocks * MOE_BLOCK, jnp.int32).at[dest].set((order // TOP_K).astype(jnp.int32))
    slot_gate = jnp.zeros(n_blocks * MOE_BLOCK, h.dtype).at[dest].set(flat_g[order].astype(h.dtype))
    block_e = jnp.minimum(jnp.searchsorted(pends, jnp.arange(n_blocks) * MOE_BLOCK, side='right'),
                          N_EXPERTS - 1)
    xs = h[slot_tok].reshape(n_blocks, MOE_BLOCK, d_)

    def run(args):
        xb, e = args
        return (jax.nn.silu(xb @ w1[e]) * (xb @ w3[e])) @ w2[e]

    ys = lax.map(run, (xs, block_e)).reshape(-1, d_)
    return jnp.zeros_like(h).at[slot_tok].add(ys * slot_gate[:, None])

def second_inputs(seed: int = 0) -> dict:
    key = jax.random.key(seed)
    ks = jax.random.split(key, 23)

    def nrm(k, shape, s):
        return jax.random.normal(k, shape, jnp.float32) * s

    d = D_MODEL
    return {
        'x': nrm(ks[0], (BATCH, SEQ, d), 1.0),
        'c': nrm(ks[1], (BATCH, d), 1.0),
        'ctx': nrm(ks[2], (BATCH, CTX_LEN, d), 1.0),
        'c_ctx': nrm(ks[3], (d,), 1.0),
        'w_ada': nrm(ks[4], (DEPTH, d, 6 * d), d ** -0.5),
        'b_ada': nrm(ks[5], (DEPTH, 6 * d), 0.02),
        'w_in': nrm(ks[6], (DEPTH, d, IN_WIDTH), d ** -0.5),
        'conv_w': nrm(ks[7], (DEPTH, 3, CONV_WIDTH_2), 3 ** -0.5),
        'attn_sink': nrm(ks[8], (DEPTH, N_HEADS), 0.5),
        'gm_ws': nrm(ks[9], (DEPTH, GM_GROUPS, CHUNK, CHUNK), CHUNK ** -0.5),
        'gm_bs': 1.0 + nrm(ks[10], (DEPTH, GM_GROUPS, CHUNK), 0.02),
        'w_out': nrm(ks[11], (DEPTH, MIX_WIDTH, d), BETA * MIX_WIDTH ** -0.5),
        'ln1_g': 1.0 + nrm(ks[12], (DEPTH, d), 0.02),
        'ln1_b': nrm(ks[13], (DEPTH, d), 0.02),
        'w_rg': nrm(ks[14], (DEPTH, d, N_GROUPS), d ** -0.5),
        'b_rg': nrm(ks[15], (DEPTH, N_GROUPS), 0.01),
        'w_re': nrm(ks[16], (DEPTH, d, N_EXPERTS), d ** -0.5),
        'b_re': nrm(ks[17], (DEPTH, N_EXPERTS), 0.01),
        'w1': nrm(ks[18], (DEPTH, N_EXPERTS, d, D_EXPERT), d ** -0.5),
        'w3': nrm(ks[19], (DEPTH, N_EXPERTS, d, D_EXPERT), d ** -0.5),
        'w2': nrm(ks[20], (DEPTH, N_EXPERTS, D_EXPERT, d), BETA * D_EXPERT ** -0.5),
        'ln2_g': 1.0 + nrm(ks[21], (DEPTH, d), 0.02),
        'ln2_b': nrm(ks[22], (DEPTH, d), 0.02),
    }

def second_block(x, c, ctx, c_ctx, w_ada, b_ada, w_in, conv_w, attn_sink, gm_ws, gm_bs, w_out,
              ln1_g, ln1_b, w_rg, b_rg, w_re, b_re, w1, w3, w2, ln2_g, ln2_b):
    b_, s_, d_ = x.shape
    c_len = ctx.shape[1]
    rows = s_ // GRID_W
    row = jnp.repeat(jnp.arange(rows), GRID_W)
    col = jnp.tile(jnp.arange(GRID_W), rows)
    c_act = jax.nn.silu(c)
    cc_act = jax.nn.silu(c_ctx)

    for l in range(DEPTH):
        last = l == DEPTH - 1
        mod_x = c_act @ w_ada[l] + b_ada[l]
        sh1, sc1, g1, sh2, sc2, g2 = jnp.split(mod_x[:, None, :], 6, axis=-1)
        n_mod = 2 if last else 6
        mod_c = (cc_act @ w_ada[l][:, :n_mod * d_] + b_ada[l][:n_mod * d_]).reshape(n_mod, d_)

        hx = x * (1 + sc1) + sh1
        hc = ctx * (1 + mod_c[1]) + mod_c[0]
        qx, kx, vx, cbx, ccx, cvx, gux, gvx = jnp.split(hx @ w_in[l], SPLIT_POINTS, axis=-1)
        qx = axial_rope(qx.reshape(b_, s_, N_HEADS, HEAD_DIM), row, col)
        kx = axial_rope(kx.reshape(b_, s_, N_KV_HEADS, HEAD_DIM), row, col)
        vx = vx.reshape(b_, s_, N_KV_HEADS, HEAD_DIM)
        if last:
            kc, vc = jnp.split(hc @ w_in[l][:, ATTN_WIDTH:ATTN_WIDTH + 2 * KV_WIDTH], 2, axis=-1)
        else:
            qc, kc, vc, cbc, ccc, cvc, guc, gvc = jnp.split(hc @ w_in[l], SPLIT_POINTS, axis=-1)
        kc = kc.reshape(b_, c_len, N_KV_HEADS, HEAD_DIM)
        vc = vc.reshape(b_, c_len, N_KV_HEADS, HEAD_DIM)

        att_x = window_attention(qx, kx, vx, kc, vc, attn_sink[l])
        o_x = jnp.concatenate(
            [att_x, local_mixers(cbx, ccx, cvx, gux, gvx, conv_w[l], gm_ws[l], gm_bs[l])], axis=-1) @ w_out[l]
        if not last:
            att_c = context_attention(qc, kc, vc, attn_sink[l])
            o_c = jnp.concatenate(
                [att_c, local_mixers(cbc, ccc, cvc, guc, gvc, conv_w[l], gm_ws[l], gm_bs[l])], axis=-1) @ w_out[l]
            ctx = layer_norm(ALPHA * ctx + mod_c[2] * o_c, ln1_g[l], ln1_b[l])
        x = layer_norm(ALPHA * x + g1 * o_x, ln1_g[l], ln1_b[l])

        hx = (x * (1 + sc2) + sh2).reshape(b_ * s_, d_)
        if last:
            tokens = hx
        else:
            hc = (ctx * (1 + mod_c[4]) + mod_c[3]).reshape(b_ * c_len, d_)
            tokens = jnp.concatenate([hx, hc], axis=0)
        y = hier_moe(tokens, w_rg[l], b_rg[l], w_re[l], b_re[l], w1[l], w3[l], w2[l])
        if not last:
            ctx = layer_norm(ALPHA * ctx + mod_c[5] * y[b_ * s_:].reshape(b_, c_len, d_), ln2_g[l], ln2_b[l])
        x = layer_norm(ALPHA * x + g2 * y[:b_ * s_].reshape(b_, s_, d_), ln2_g[l], ln2_b[l])

    return x


def setup_inputs(seed=0):
    out = dict(first_inputs(seed))
    for name, value in second_inputs(seed + 1).items():
        if name != "x":
            out[name + "_2"] = value
    return out


def reference(
    x, positions, conv_norm, conv_w_in, conv_dw_w, conv_dw_b, conv_ln_g, conv_ln_b, conv_w_out,
    ret_norm, ret_w_in, ret_w_out, final_norm, c_2, ctx_2, c_ctx_2, w_ada_2, b_ada_2, w_in_2,
    conv_w_2, attn_sink_2, gm_ws_2, gm_bs_2, w_out_2, ln1_g_2, ln1_b_2, w_rg_2, b_rg_2, w_re_2,
    b_re_2, w1_2, w3_2, w2_2, ln2_g_2, ln2_b_2,
):
    x = first_block(
        x, positions, conv_norm, conv_w_in, conv_dw_w, conv_dw_b, conv_ln_g, conv_ln_b,
        conv_w_out, ret_norm, ret_w_in, ret_w_out, final_norm,
    )
    return second_block(
        x, c_2, ctx_2, c_ctx_2, w_ada_2, b_ada_2, w_in_2, conv_w_2, attn_sink_2, gm_ws_2,
        gm_bs_2, w_out_2, ln1_g_2, ln1_b_2, w_rg_2, b_rg_2, w_re_2, b_re_2, w1_2, w3_2, w2_2,
        ln2_g_2, ln2_b_2,
    )


_drawn_inputs = setup_inputs


def setup_inputs(seed=0):
    import zlib

    import numpy as np

    out = dict(_drawn_inputs(seed))
    spreads = {}
    factors = {'attn_sink_2': 8.0, 'gm_bs_2': 8.0, 'b_rg_2': 5.139, 'b_re_2': 5.978}
    for name, (base, spread) in spreads.items():
        noise = np.random.default_rng([zlib.crc32(name.encode()), seed]).standard_normal(out[name].shape)
        drawn = base * np.exp(spread * noise) if base else spread * noise
        out[name] = __import__('jax').numpy.asarray(drawn.astype(out[name].dtype))
    for name, factor in factors.items():
        out[name] = (out[name] * factor).astype(out[name].dtype)
    return out
```

```python
from contextlib import ExitStack

import concourse.bass as bass
import numpy as np
from concourse import mybir

ALU = mybir.AluOpType
ACT = mybir.ActivationFunctionType
AX = mybir.AxisListType
F32 = mybir.dt.float32
I32 = mybir.dt.int32

P = 128
D = 1024
KD = D // P
S = 512
C = 256
TX, TC = S // P, C // P
T = TX + TC
DI = 2 * D
KI = DI // P
TAPS = 31
RH, RQK, RV = 4, 256, 512
AH, KVH, HD = 8, 2, 64
NG, EPG = 4, 8
E = NG * EPG
DE = 512
KE = DE // P
EPS = 1e-6
LN_EPS = 1e-6
ALPHA = 4 ** 0.25
SCALE = HD ** -0.5
CW = 512
CHUNK = KD * CW
BIG = 1e30
LAYERS = 2

RING = 0
FREE2 = 3 * CHUNK
XRES = 6 * CHUNK
TAB = XRES + T * D
TAB_N = 1088
SMALL = TAB + TAB_N
SMALL_N = 1024
W0 = SMALL + SMALL_N
W0_N = 18432
ARENA = W0 + W0_N

T_ID, T_TRI, T_BAND, T_ROPE, T_FREQ = 0, 128, 256, 640, 896
T_EI, T_BI, T_TOK = 897, 929, 977
V_CW, V_LNG, V_LNB, V_CN, V_RN, V_C, V_SC, V_GB = 0, 512, 528, 544, 552, 560, 576, 588
V_N = 596
V_SINK, V_RB, V_ST = 596, 612, 700


def tables():
    t = np.zeros((P, TAB_N), np.float32)
    i = np.arange(P)
    t[:, T_ID:T_ID + P] = np.eye(P)
    t[:, T_TRI:T_TRI + P] = i[:, None] < i[None, :]
    band = np.zeros((P, 3 * P), np.float32)
    band[:, :P] = np.where(i[None, :] >= i[:, None], 0.0, -BIG)
    band[:, 2 * P:] = np.where(i[None, :] <= i[:, None], 0.0, -BIG)
    t[:, T_BAND:T_BAND + 3 * P] = band
    m = HD // 4
    freqs = (np.float32(10000.0) ** (-np.arange(m, dtype=np.float32) / np.float32(m))).astype(np.float32)
    tok = np.arange(S)
    ang = np.stack([(tok // 64).astype(np.float32)[:, None] * freqs,
                    (tok % 64).astype(np.float32)[:, None] * freqs], 1)
    rope = np.stack([np.cos(ang), np.sin(ang)], 1).reshape(TX, P, 4 * m)
    t[:, T_ROPE:T_ROPE + 256] = rope.transpose(1, 0, 2).reshape(P, 256)
    h = RQK // 2
    t[:, T_FREQ] = (np.float32(10000.0) ** (-np.arange(h, dtype=np.float32) / np.float32(h))).astype(np.float32)
    t[:, T_EI:T_EI + E] = np.arange(E)
    t[:, T_BI:T_BI + 48] = np.arange(48)
    t[:, T_TOK:T_TOK + T] = i[:, None] + P * np.arange(T)[None, :]
    lg = np.log(1.0 - 2.0 ** (-5.0 - np.arange(RH, dtype=np.float64)))
    diff = np.arange(S)[None, None, :] - i[:, None, None]
    decay = np.where(diff >= 0, np.exp(np.maximum(diff, 0) * lg[None, :, None]), 0.0) * RQK ** -0.5
    lower = np.broadcast_to((np.arange(E)[None, :] < np.arange(E)[:, None]).astype(np.float32), (P, E, E))
    return t, decay.astype(np.float32).reshape(P, RH * S), np.ascontiguousarray(lower).reshape(P, E * E)


def build(nc, a, out, stop=None):
    ctx = ExitStack()
    with ctx:
        arena = ctx.enter_context(nc.sbuf_tensor("arena", [P, ARENA], F32))
        psum = ctx.enter_context(nc.psum_tensor("psum", [P, 8 * 512], F32))
        made = {}

        def sem(name):
            if name not in made:
                made[name] = ctx.enter_context(nc.semaphore(name))
            return made[name]

        def mem(at, n, parts=P):
            return arena[0:parts, at:at + n]

        def mem3(at, n, m, parts=P):
            return arena[0:parts, at:at + n * m].rearrange("p (n m) -> p n m", n=n)

        def bank(b, n=512, at=0):
            return psum[:, b * 512 + at:b * 512 + at + n]

        def bcast(ap, parts=P):
            return ap.partition_broadcast(parts)

        ident = mem(TAB + T_ID, P)
        tri = mem(TAB + T_TRI, P)
        xr = mem3(XRES, T, D)
        small = mem(SMALL, SMALL_N)
        stats = mem(SMALL + V_ST, SMALL_N - V_ST)

        mod = nc.dram_tensor("mod_rows", (LAYERS, 2, 6 * D), F32, kind="Internal").ap()

        c_hT = mem3(FREE2, KD, S)
        c_z = FREE2 + CHUNK
        c_xn = mem3(FREE2 + CHUNK, TX, D)
        c_c = W0
        c_up = [mem(W0 + 8192 + 544 * k, 544) for k in range(2)]
        c_acc = [[mem(W0 + 9280 + 1024 * k + 512 * j, S) for j in range(2)] for k in range(2)]
        c_sg = [mem(W0 + 11328 + 512 * k, S) for k in range(2)]
        c_sum = mem(W0 + 12352, S)
        c_sq = mem(W0 + 12864, S)
        c_mean = mem(W0 + 13376, S)
        c_rstd = mem(W0 + 13888, S)
        c_tmp = [mem(W0 + 14400 + 512 * k, S) for k in range(2)]
        c_tmp2 = [mem(W0 + 15424 + 512 * k, S) for k in range(2)]
        c_ones = mem(W0 + 16448, P)
        c_wb = [mem(W0 + 16576 + 32 * k, 32) for k in range(2)]
        a_bias = [mem(W0 + 6 * D * l, 6 * D, 2) for l in range(LAYERS)]
        a_row = [mem(FREE2 + 2 * CHUNK + 1024 * k, CW, 2) for k in range(3)]
        a_c = mem(SMALL + V_C, 16)
        r_q = FREE2 + CHUNK
        r_k = FREE2 + 2 * CHUNK
        r_v = mem3(W0, TX, DI)
        r_g = W0 + 8192
        r_xn = mem3(W0, TX, D)
        r_decay = mem3(W0 + 16384, RH, S)
        r_cos, r_sin = mem(XRES + TX * D, S), mem(XRES + TX * D + S, S)
        r_t = [mem(XRES + TX * D + 1024 + 512 * k, S) for k in range(2)]
        r_pos = mem(FREE2 + CHUNK, S)
        r_posf, r_ang = mem(FREE2 + CHUNK + 512, S), mem(FREE2 + CHUNK + 1024, S)
        r_n = [mem(FREE2 + CHUNK + 1536 + 512 * k, S) for k in range(2)]
        r_s = [mem(FREE2 + o, S - P * j) for j, o in enumerate((0, 512, 896, 1152))]
        r_on = mem3(FREE2 + 1280, TX, RV)
        r_junk = mem(FREE2 + 3328, RV)
        f_g = mem(W0, D)

        b_hxT = mem3(FREE2, KD, T * P)
        b_hx = mem3(FREE2 + 6144, T, D)
        b_att = mem3(FREE2, AH // 2, T * P)
        b_gmT = mem3(FREE2 + 3072, 2, T * P)
        b_qT = mem3(FREE2 + 6144, AH // 2, T * P)
        b_kT = mem3(FREE2 + 9216, KVH, T * P)
        b_cv = mem3(FREE2 + 10752, 2, T * P)
        b_mod = [mem(W0 + D * j, D) for j in range(6)]
        b_ln = [mem(W0 + 6144 + D * j, D) for j in range(2)]
        b_wsT = mem3(W0 + 4096, 4, P)
        b_acc = W0 + 4608
        b_t = [mem(W0 + 5376 + 256 * j, 256) for j in range(2)]
        b_tk = mem(W0 + 5888, KVH * HD)
        b_q = mem3(W0 + 8192, T, AH * HD)
        b_k = mem3(W0 + 11264, T, 2 * KVH * HD)
        b_v = mem3(W0 + 12800, T, KVH * HD)
        b_g = mem3(W0 + 13568, T, 512)
        UPAD = S + 2 + C + 2
        b_u = mem3(W0 + 16640, 2, UPAD)
        b_sb = [mem3(W0 + 2560 * j, 4, 640) for j in range(2)]
        b_pT = mem3(W0 + 8192, 5, 512)
        b_tmp = mem(W0 + 8192, D)
        o_wr = W0 + 9216
        b_wr = mem3(o_wr, KD, NG + E)
        o_r = W0 + 9728
        g_lower = mem3(o_r, E, E)
        g_prod = mem3(o_r + 1024, E, E)
        g_lg = o_r + 2048
        g_a = [o_r + 2272 + 224 * j for j in range(6)]
        g_s = o_r + 3616
        g_be = mem(o_r + 3936, 48).bitcast(I32)
        g_n = [mem(SMALL + V_ST + 264 + 8 * l, 8).bitcast(I32) for l in range(LAYERS)]
        g_cmp = mem3(W0 + 13824, 48, E, 1)
        g_rows = mem3(W0 + 15872, P, 2).bitcast(I32)
        g_rowf = mem3(W0 + 16128, P, 2)
        g_idx = mem3(W0 + 16384, 2, 48).bitcast(I32)
        g_init = mem3(W0 + 16480, 48, 2).bitcast(I32)
        g_dest = [mem(W0 + 16576 + 8 * k, 8).bitcast(I32) for k in range(2)]
        g_ids = mem3(W0 + 16592, T * 2, 2).bitcast(I32)
        g_ones = mem(W0 + 16640, P)
        g_gate = [mem(W0 + 16768 + 8 * k, 8) for k in range(2)]
        m_xs = [mem(W0 + 2048 + D * j, D) for j in range(2)]
        m_xsT = [mem3(W0 + 4096 + D * j, KD, P) for j in range(2)]
        m_sg, m_h = mem(W0 + 8192, DE), mem(W0 + 8704, DE)
        m_hT = mem3(W0 + 9216, KE, P)
        m_y = [mem(W0 + 13824 + D * j, D) for j in range(2)]
        m_gi = [mem(W0 + 16784 + 8 * j, 1).bitcast(I32) for j in range(2)]
        m_si = [mem(W0 + 16800 + 8 * j, 1).bitcast(I32) for j in range(2)]
        c_y = [mem3(FREE2 + 2048 * t if t < 3 else W0 + 10240 + 2048 * (t - 3), 2, D) for t in range(T)]

        def full(l):
            return list(range(T)) if l == 0 else list(range(TX))

        NBL = [2 * len(full(l)) * P // P + E for l in range(LAYERS)]
        moe_in = [nc.dram_tensor(f"moe_in{l}", (len(full(l)) * P, D), F32, kind="Internal").ap() for l in range(LAYERS)]
        slot_tok = [nc.dram_tensor(f"slot_tok{l}", ((NBL[l] + 2) * P, 2), I32, kind="Internal").ap()
                    for l in range(LAYERS)]
        moe_out = [nc.dram_tensor(f"moe_out{l}", (2 * len(full(l)) * P, D), F32, kind="Internal").ap()
                   for l in range(LAYERS)]

        def in_outputs(l):
            parts = [0, 1] if l == 0 else [0]
            o = [(0, "q", t, "dve") for t in full(l)]
            o += [(1, "kv", t, "dve") for t in range(T)]
            o += [(1, "cb", (f, s_), "act") for f in range(2) for s_ in parts]
            o += [(2, "cc", (f, s_), "act") for f in range(2) for s_ in parts]
            o += [(2, "cx", (f, s_), "dve") for f in range(2) for s_ in parts]
            o += [(3, "g", t, "act") for t in full(l)]
            return o

        def taken(outs, n, who):
            return sum(o[3] == who for o in outs[:n + 1])

        RANGE = [(0, S, 1), (S, C, S + 3)]

        def att_units(l):
            u = []
            for n in full(l):
                lo, hi = (max(n - 1, 0), min(n + 1, TX - 1)) if n < TX else (0, -1)
                u += [(n, lo, hi, kv) for kv in range(KVH)]
            return u

        def local_done(units, u, hh):
            before = sum(4 for x in units[:u] if x[2] >= x[1])
            return before + (hh + 1 if units[u][2] >= units[u][1] else 0)

        def at_t_before(units, u):
            return sum(x[2] - x[1] + 1 + TC for x in units[:u])

        def at_half_before(units, u, odd):
            return sum((x[2] - x[1] + 1 + TC + 1 - odd) // 2 for x in units[:u])

        def chain(eng, name):
            n = [0]
            s = sem(name)

            def link(ins):
                n[0] += 1
                ins.then_inc(s, 1)
                eng.wait_ge(s, n[0])
            return link

        u0, o0 = att_units(0), in_outputs(0)
        U0 = len(u0)
        TOTAL = {
            "at_c": 4 * U0, "at_e": 5 * U0, "at_l": local_done(u0, U0 - 1, 3), "at_m": U0, "at_o": 2 * U0,
            "at_pv": U0, "at_p": U0, "at_s": 4 * U0, "at_ta": at_half_before(u0, U0, 0),
            "at_td": at_half_before(u0, U0, 1), "at_t": at_t_before(u0, U0), "cv_y": 4, "dest": 3, "gmT": 4,
            "gm_mm": T, "gm_sd": 1, "gm_t": 1, "gm_ve": 1, "gm_y": T, "gv": T, "idx": 2,
            "in_act": taken(o0, len(o0), "act"), "in_dve": taken(o0, len(o0), "dve"), "in_mm": len(o0),
            "kT": T, "kt": T, "lg_mm": T, "ob_mm": 2 * T, "ob_x": 2 * T, "qT": T, "qt": T, "rank": 2,
            "rt_M": 1, "rt_act": 2, "rt_dve": 2, "upad": 1,
            "meta": 1, "wr": 32, "ws": 16, "hx2_out": 16 * T,
        }

        TOTAL |= {"rms_ss": 1, "rms_ms": 1, "rms_sd": 1, "rms_xn": TX, "rms_tp": KD, "rms_hT": KD,
                  "op_mm": 8, "op_chunk": 3, "op_x": 8, "hx_t": T, "hx_Ta": T, "hx_Td": T, "hx_in": T,
                  "mod_in": 16 * 12, "tok0": 32, "tok": 32 * T}

        def past(name, rounds):
            return TOTAL[name] * rounds

        def past_rows(q):
            return T * min(q, 2) + TX * max(q - 2, 0)

        def mod_order(q):
            return [4, 5, 0, 1, 2, 3] if q == 0 else list(range(T)) if q < 3 else list(range(TX))

        def mod_bank(q, i_):
            return 2 * (i_ % (4 if q % 2 == 0 else 2))

        def done_before(eng, l):
            if l == 0:
                return 0, (0, 0)
            return (eng.value_load(g_n[0][0:1, 0:1], min_val=2, max_val=NBL[0]),
                    tuple(eng.value_load(g_n[0][0:1, 1 + p:2 + p], min_val=16, max_val=16 * NBL[0]) for p in range(2)))

        stream = []

        def chunk_cols(w, n):
            return w.rearrange("(k p) n -> p k n", p=P)[:, :, n * CW:(n + 1) * CW]

        def chunk_rows(w, n):
            return w.rearrange("(k p) n -> p k n", p=P)[:, 4 * n:4 * n + 4, :]

        stream_done = []
        for n in range(4):
            stream.append(chunk_rows(a["conv_w_out"], n))
            stream_done.append(("op_mm", 8) if n == 3 else ("op_chunk", n + 1))
        S_RIN = len(stream)
        for n in range(12):
            stream.append(chunk_cols(a["ret_w_in"], n))
            stream_done.append(("ri_mm", 4 * n + 4))
        S_ROUT = len(stream)
        for n in range(4):
            stream.append(chunk_rows(a["ret_w_out"], n))
            stream_done.append(("op_mm", past("op_mm", 1) + 8) if n == 3 else ("op_chunk", past("op_chunk", 1) + n + 1))
        S_B2 = []
        for l in range(LAYERS):
            S_B2.append(len(stream))
            for n in range(4):
                stream.append(chunk_cols(a["w_in"][l], n))
                stream_done.append(("in_mm", past("in_mm", l) + sum(o[0] <= n for o in in_outputs(l))))
            for n in range(2):
                stream.append(chunk_rows(a["w_out"][l], n))
                stream_done.append(("ob_mm", past("ob_mm", l) + 2 * len(full(l))))

        def slot(n):
            return mem(RING + CHUNK * (n % 3), CHUNK)

        def slot_cols(n):
            return slot(n).rearrange("p (k c) -> p k c", k=KD)

        def slot_rows(n):
            return slot(n).rearrange("p (k c) -> p k c", k=4)

        block = ctx.enter_context(nc.Block())

        @block.sync
        def _(sp):
            sp.dma_start(mem(TAB, TAB_N), a["tab"]).then_inc(sem("const_in"), 16)
            sp.dma_start(mem(SMALL, V_N), a["vec"]).then_inc(sem("const_in"), 16)
            wa = [a["w_ada"][l].rearrange("(k p) n -> p k n", p=P) for l in range(LAYERS)]

            def ada(l, s, cols):
                sp.dma_start(slot_cols(s), wa[l][:, :, cols]).then_inc(sem(f"st_w{s}"), 16)

            for s in range(3):
                ada(0, s, slice(s * CW, (s + 1) * CW))
                if s == 0:
                    for l in range(LAYERS):
                        sp.dma_start(a_bias[l], bcast(a["b_ada"][l], 2)).then_inc(sem("x_in"), 16)
                    for t in range(TX):
                        sp.dma_start(xr[:, t, :], a["x"][t * P:(t + 1) * P, :]).then_inc(sem("x_in"), 16)
            with sp.Fori(1, 4) as i:
                for s in range(3):
                    sp.wait_ge(sem("ada_mm"), 3 * i + (s - 2))
                    ada(0, s, bass.ds(i * (3 * CW) + s * CW, CW))
            with sp.Fori(0, 4) as i:
                for s in range(3):
                    sp.wait_ge(sem("ada_mm"), 3 * i + (s + 10))
                    ada(1, s, bass.ds(i * (3 * CW) + s * CW, CW))

            wc = a["conv_w_in"].rearrange("(k p) n -> p k n", p=P)

            def group(s, col):
                for role in range(3):
                    sp.dma_start(mem3(RING + 6144 * s + 2048 * role, KD, 256),
                                 wc[:, :, bass.ds(role * DI + col, 256)]).then_inc(sem(f"cv_w{s}"), 16)

            sp.wait_ge(sem("ada_mm"), 24)
            group(0, 0)
            group(1, 256)
            with sp.Fori(1, 4) as i:
                for s in range(2):
                    sp.wait_ge(sem("cv_z"), 4 * i + (2 * s - 2))
                    group(s, i * 512 + s * 256)

            def load(n):
                if n == 0:
                    sp.wait_ge(sem("cv_z"), KI)
                elif n >= 3:
                    name, count = stream_done[n - 3]
                    sp.wait_ge(sem(name), count)
                sp.dma_start(slot(n).rearrange("p (k c) -> p k c", k=stream[n].shape[1]), stream[n])\
                    .then_inc(sem(f"st_w{n % 3}"), 16)

            for n in range(S_RIN):
                load(n)
            for n in range(S_RIN, S_ROUT):
                if n == S_RIN + 1:
                    sp.wait_ge(sem("op_mm"), past("op_mm", 0) + 8)
                    sp.wait_ge(sem("y_ready"), KI)
                    sp.dma_start(r_pos.bitcast(I32), bcast(a["positions"][0])).then_inc(sem("pos_in"), 16)
                    sp.dma_start(mem(W0 + 16384, RH * S), a["decay"]).then_inc(sem("pos_in"), 16)
                load(n)
            for n in range(S_ROUT, S_ROUT + 4):
                load(n)
            for l in range(LAYERS):
                sp.dma_start(mem(SMALL + V_SINK + AH * l, AH), bcast(a["attn_sink"][l])).then_inc(sem("rows_in"), 16)
                sp.dma_start(mem(SMALL + V_RB + (NG + E) * l, NG + E), bcast(a["b_router"][l]))\
                    .then_inc(sem("rows_in"), 16)
            sp.wait_ge(sem("ri_dve"), 16)
            for t in range(TC):
                sp.dma_start(xr[:, TX + t, :], a["ctx"][t * P:(t + 1) * P, :]).then_inc(sem("ctx_in"), 16)
            sp.wait_ge(sem("ra_o"), RH * TX)
            sp.dma_start(f_g, bcast(a["final_norm"])).then_inc(sem("fg_in"), 16)

            if stop == 1:
                sp.wait_ge(sem("fin_x"), TX)
                for t in range(TX):
                    sp.dma_start(out[t * P:(t + 1) * P, :], xr[:, t, :]).then_inc(sem("out"), 16)
                sp.wait_ge(sem("out"), 16 * TX)
                return

            def mod_row(l, who, j, place):
                sp.dma_start(b_mod[place], bcast(mod[l][who][j * D:(j + 1) * D])).then_inc(sem("mod_in"), 16)

            def first_rows(l):
                for who, j, place in ((1, 0, 4), (1, 1, 5), (0, 0, 2), (0, 1, 3)):
                    mod_row(l, who, j, place)

            for s in range(3):
                sp.wait_ge(sem(f"ada_out{s}"), 16 * 8)
            first_rows(0)
            for l in range(LAYERS):
                base = S_B2[l]
                nt = len(full(l))
                sp.wait_ge(sem("hx_in"), past("hx_in", 2 * l) + T)
                sp.dma_start(b_wsT, a["gm_wsT"][l]).then_inc(sem("ws"), 16)
                for j, k in enumerate(("ln1_g", "ln1_b")):
                    sp.dma_start(b_ln[j], bcast(a[k][l])).then_inc(sem("row_w"), 16)
                for n in range(base if l == 0 else base + 3, base + 6):
                    load(n)
                units = att_units(l)
                sp.wait_ge(sem("at_o"), past("at_o", l) + 2 * len(units))
                for who in ((0, 1) if l == 0 else (0,)):
                    for i_, j in enumerate((2, 4, 3)):
                        mod_row(l, who, j, 3 * who + i_)
                sp.dma_start(b_wr, a["w_router"][l].rearrange("(k p) n -> p k n", p=P)).then_inc(sem("wr"), 16)
                sp.dma_start(mem(o_r, E * E), a["lower"]).then_inc(sem("wr"), 16)
                sp.wait_ge(sem("hx_in"), past("hx_in", 2 * l + 1) + nt)
                for who in ((0, 1) if l == 0 else (0,)):
                    mod_row(l, who, 5, who)
                for j, k in enumerate(("ln2_g", "ln2_b")):
                    sp.dma_start(b_ln[j], bcast(a[k][l])).then_inc(sem("row_w"), 16)
                sp.wait_ge(sem("ob_mm"), past("ob_mm", l) + 2 * nt)
                sp.wait_ge(sem("lg_mm"), past("lg_mm", l) + nt)
                sp.wait_ge(sem("hx2_out"), past("hx2_out", l) + 16 * nt)
                sp.wait_ge(sem("meta"), past("meta", l) + 1)
                count = sp.value_load(g_n[l][0:1, 0:1], min_val=2, max_val=NBL[l])
                nb0, rows0 = done_before(sp, l)
                ws = [a[k][l].rearrange("e (k p) n -> p (e k) n", p=P) for k in ("w1", "w3", "w2")]
                kk = (KD, KD, KE)
                with sp.Fori(0, NBL[l] // 2) as i:
                    for p in range(2):
                        with sp.If(2 * i + p < count):
                            e = sp.value_load(g_be[0:1, bass.ds(2 * i + p, 1)], min_val=0, max_val=E - 1)
                            for j, used in enumerate(("m_w1", "m_w3", "m_w2")):
                                sp.wait_ge(sem(used), nb0 + 2 * i + (p + 1))
                                if (p, j) == (0, 2):
                                    sp.sem_inc(sem("settled"), 1)
                                    sp.wait_ge(sem("m_g0"), rows0[0] + (16 * l + 16))
                                    sp.sem_inc(sem("settled"), 1)
                                sp.dma_start(mem(RING + CHUNK * (3 * p + j), CHUNK)
                                             .rearrange("p (k c) -> p k c", k=kk[j]),
                                             ws[j][:, bass.ds(e * kk[j], kk[j]), :])\
                                    .then_inc(sem(f"m_load{3 * p + j}"), 16)
                sp.wait_ge(sem("m_done"), l + 1)
                for t in full(l):
                    sp.dma_start(c_y[t], moe_out[l][2 * P * t:2 * P * (t + 1), :].rearrange("(p k) d -> p k d", k=2))\
                        .then_inc(sem(f"cg{t}"), 16)
                if l + 1 < LAYERS:
                    sp.wait_ge(sem("mod_in"), past("mod_in", l) + 64 + 64 * (2 - l))
                    first_rows(l + 1)
                    for n in range(S_B2[l + 1], S_B2[l + 1] + 3):
                        load(n)
            for t in range(TX):
                sp.wait_ge(sem("row_x"), past_rows(3) + t + 1)
                sp.dma_start(out[t * P:(t + 1) * P, :], xr[:, t, :]).then_inc(sem("out"), 16)
            sp.wait_ge(sem("out"), 16 * TX)

        @block.scalar
        def _(act):
            link = chain(act, "act_chain")
            act.sem_inc(sem("m_ya"), 1)

            def sum_squares(r, junk, ready):
                for t in range(TX):
                    ready(t)
                    link(act.activation(junk, xr[:, t, :], ACT.Square, accum_out=stats[:, t:t + 1]))
                act.activation(stats[:, 4:5], stats[:, 0:1], ACT.Copy).then_inc(sem("rms_ss"), 1)

            def root(r):
                act.wait_ge(sem("rms_ms"), past("rms_ms", r) + 1)
                act.activation(stats[:, 8:12], stats[:, 0:4], ACT.Sqrt).then_inc(sem("rms_sd"), 1)

            def gain(r, hT, g):
                for k in range(KD):
                    act.wait_ge(sem("rms_tp"), past("rms_tp", r) + k + 1)
                    act.activation(hT[:, k, :], bank(6 + k % 2), ACT.Copy, scale=small[:, g + k:g + k + 1])\
                        .then_inc(sem("rms_hT"), 1)

            act.wait_ge(sem("const_in"), 32)
            act.activation(mem(SMALL + V_ST + 40, 16), a_c, ACT.Silu).then_inc(sem("c_act"), 1)
            sum_squares(0, mem(FREE2, D), lambda t: act.wait_ge(sem("x_in"), 16 * (LAYERS + TX)) if t == 0 else None)
            root(0)
            gain(0, c_hT, V_CN)

            act.sem_inc(sem("cv_act_free"), 2)
            with act.Fori(0, KI // 2) as i:
                for p in range(2):
                    act.wait_ge(sem("cv_b"), 2 * i + (p + 1))
                    act.wait_ge(sem("cv_dve_free"), 2 * i + (p + 1))
                    act.activation(c_sg[p], bank(2 + p), ACT.Sigmoid).then_inc(sem("cv_sg"), 1)
                    act.wait_ge(sem("cv_z"), 2 * i + (p + 1))
                    act.activation(arena[:, bass.ds(i * 1024 + (c_z + 512 * p), S)], bank(4 + p), ACT.Silu)\
                        .then_inc(sem("cv_act_free"), 1)

            act.wait_ge(sem("ln_mm"), 1)
            act.activation(c_mean, bank(6), ACT.Copy).then_inc(sem("ln_act"), 1)
            act.sem_inc(sem("ln_sqadd"), 2)
            with act.Fori(0, KI // 2) as i:
                for p in range(2):
                    act.wait_ge(sem("ln_d"), 2 * i + (p + 1))
                    act.wait_ge(sem("ln_sqadd"), 2 * i + (p + 1))
                    act.activation(c_tmp[p], arena[:, bass.ds(i * 1024 + (c_c + 512 * p), S)], ACT.Square)\
                        .then_inc(sem("ln_sq"), 1)
            act.wait_ge(sem("ln_ve"), 1)
            act.activation(c_rstd, c_sq, ACT.Sqrt).then_inc(sem("ln_act"), 1)
            with act.Fori(0, KI // 2) as i:
                for p in range(2):
                    act.wait_ge(sem("ln_n"), 2 * i + (p + 1))
                    act.wait_ge(sem("y_ready_tok"), 2 * i + (p + 1))
                    act.activation(c_tmp2[p], c_tmp[p], ACT.Silu,
                                   bias=small[:, bass.ds(i * 2 + (V_LNB + p), 1)],
                                   scale=small[:, bass.ds(i * 2 + (V_LNG + p), 1)]).then_inc(sem("ln_s"), 1)

            sum_squares(1, mem(FREE2, D), lambda t: act.wait_ge(sem("op_x"), past("op_x", 0) + 2 * (t + 1)))
            root(1)
            gain(1, c_hT, V_RN)
            act.wait_ge(sem("rot_arg"), 1)
            act.activation(r_cos, r_cos, ACT.Sin).then_inc(sem("rot"), 1)
            act.activation(r_sin, r_sin, ACT.Sin).then_inc(sem("rot"), 1)
            for n in range(4, 12):
                for j in range(4):
                    act.wait_ge(sem("ri_mm"), 4 * n + j + 1)
                    b = bank(4 * (n % 2) + j)
                    if n < 8:
                        act.activation(r_v[:, j, (n - 4) * CW:(n - 3) * CW], b, ACT.Copy)\
                            .then_inc(sem("ri_act"), 1)
                    else:
                        act.activation(mem(r_g + S * (4 * (n - 8) + j), S), b, ACT.Silu)\
                            .then_inc(sem("ri_act"), 1)
            for h in range(RH):
                for t in range(TX):
                    act.wait_ge(sem("ra_o"), TX * h + t + 1)
                    link(act.activation(r_junk, bank(4 + t), ACT.Square, accum_out=stats[:, 16 + t:17 + t]))
                act.activation(stats[:, 28:29], stats[:, 16:17], ACT.Copy).then_inc(sem("ra_ss"), 1)
                act.wait_ge(sem("ra_ms"), h + 1)
                act.activation(stats[:, 24:28], stats[:, 16:20], ACT.Sqrt).then_inc(sem("ra_sd"), 1)
            sum_squares(2, mem(W0 + D, D), lambda t: act.wait_ge(sem("op_x"), past("op_x", 1) + 2 * (t + 1)))
            root(2)
            if stop == 1:
                return

            def mod_copy(q, i_):
                t = mod_order(q)[i_]
                act.wait_ge(sem("hx_t"), past("hx_t", q) + i_ + 1)
                act.activation(b_hxT[:, 0:4, t * P:(t + 1) * P],
                               bank(mod_bank(q, i_)).rearrange("p (k n) -> p k n", k=4), ACT.Copy)\
                    .then_inc(sem("hx_Ta"), 1)

            def row_root(q, i_):
                act.wait_ge(sem("row_ve"), past_rows(q) + i_ + 1)
                act.activation(stats[:, 190 + i_:191 + i_], stats[:, 184 + i_:185 + i_], ACT.Sqrt)\
                    .then_inc(sem("row_sd"), 1)

            for l in range(LAYERS):
                tiles, outs, units = full(l), in_outputs(l), att_units(l)
                nt = len(tiles)
                for i_ in range(T):
                    mod_copy(2 * l, i_)
                act.wait_ge(sem("upad"), past("upad", l) + 1)
                for n, (_, kind, w, who) in enumerate(outs):
                    if who != "act":
                        continue
                    act.wait_ge(sem("in_mm"), past("in_mm", l) + n + 1)
                    if kind == "g":
                        act.activation(b_g[:, w, :], bank(n % 8), ACT.Gelu_apprx_tanh).then_inc(sem("in_act"), 1)
                        continue
                    f, part = w
                    t0, tn, place = RANGE[part]
                    dst = b_cv[:, f, t0:t0 + tn] if kind == "cb" else b_u[:, f, place:place + tn]
                    act.activation(dst, bank(n % 8, tn), ACT.Copy).then_inc(sem("in_act"), 1)
                for i_, t in enumerate(tiles):
                    act.wait_ge(sem("qt"), past("qt", l) + i_ + 1)
                    act.activation(b_qT[:, :, t * P:(t + 1) * P], bank(6).rearrange("p (j n) -> p j n", j=4),
                                   ACT.Copy).then_inc(sem("qT"), 1)
                act.wait_ge(sem("gm_ve"), past("gm_ve", l) + 1)
                act.activation(stats[:, 190:190 + nt], stats[:, 184:184 + nt], ACT.Sqrt).then_inc(sem("gm_sd"), 1)
                act.wait_ge(sem("gm_t"), past("gm_t", l) + 1)
                for f in range(2):
                    act.activation(b_gmT[:, f, 0:S], bank(2 + f), ACT.Copy).then_inc(sem("gmT"), 1)
                    if l == 0:
                        act.activation(b_gmT[:, f, S:S + C], bank(4 + f, C), ACT.Copy).then_inc(sem("gmT"), 1)

                def context_scores(u):
                    for hh in range(4):
                        act.wait_ge(sem("at_s"), past("at_s", l) + 4 * u + hh + 1)
                        n, lo, hi, kv = units[u]
                        L = P * (hi - lo + 1)
                        act.activation(b_sb[u % 2][:, hh, L:L + C], psum[:, 1024 * (hh % 2) + 512:1024 * (hh % 2) + 768],
                                       ACT.Copy, scale=SCALE).then_inc(sem("at_c"), 1)

                def exps(u):
                    n, lo, hi, kv = units[u]
                    W = P * (hi - lo + 1) + C
                    act.wait_ge(sem("at_m"), past("at_m", l) + u + 1)
                    o = 200 + 32 * (u % 2)
                    for hh in range(4):
                        sb = b_sb[u % 2][:, hh, 0:W]
                        act.activation(sb, sb, ACT.Exp, bias=stats[:, o + 4 + hh:o + 5 + hh],
                                       accum_out=stats[:, o + 12 + hh:o + 13 + hh]).then_inc(sem("at_e"), 1)
                    act.activation(stats[:, o + 16:o + 20], stats[:, o + 8:o + 12], ACT.Exp)\
                        .then_inc(sem("at_e"), 1)

                def turned(u):
                    n, lo, hi, kv = units[u]
                    nk = hi - lo + 1 + TC
                    for c in range(0, nk, 2):
                        act.wait_ge(sem("at_t"), past("at_t", l) + at_t_before(units, u) + c + 1)
                        act.activation(b_pT[:, c, :], bank(4), ACT.Copy).then_inc(sem("at_ta"), 1)

                def attended(u):
                    n, lo, hi, kv = units[u]
                    act.wait_ge(sem("at_pv"), past("at_pv", l) + u + 1)
                    o = bank(6 + u % 2)[0:HD].rearrange("p (j a n) -> p j a n", a=2, n=P)
                    for h_ in range(2):
                        act.activation(b_att[HD * h_:HD * h_ + HD, 2 * kv:2 * kv + 2, n * P:(n + 1) * P],
                                       o[:, :, h_, :], ACT.Copy).then_inc(sem("at_o"), 1)

                context_scores(0)
                exps(0)
                for u in range(len(units)):
                    if u + 1 < len(units):
                        context_scores(u + 1)
                    turned(u)
                    if u + 1 < len(units):
                        exps(u + 1)
                    attended(u)
                for i_ in range(nt):
                    row_root(2 * l, i_)
                for i_, t in enumerate(tiles):
                    act.wait_ge(sem("hx_in"), past("hx_in", 2 * l + 1) + i_ + 1)
                    act.dma_start(moe_in[l][t * P:(t + 1) * P, :], b_hx[:, t, :]).then_inc(sem("hx2_out"), 16)
                    mod_copy(2 * l + 1, i_)
                act.wait_ge(sem("rt_dve"), past("rt_dve", l) + 1)
                ge = mem(g_s, 6 * 4)[:, 0:4 * nt]
                act.activation(ge, ge, ACT.Exp).then_inc(sem("rt_act"), 1)
                act.wait_ge(sem("rt_dve"), past("rt_dve", l) + 2)
                ed = mem(g_s + 24, 6)[:, 0:nt]
                act.activation(ed, ed, ACT.Exp).then_inc(sem("rt_act"), 1)
                act.wait_ge(sem("meta"), past("meta", l) + 1)
                count = act.value_load(g_n[l][0:1, 0:1], min_val=2, max_val=NBL[l])
                nb0, rows0 = done_before(act, l)
                act.wait_ge(sem("m_t"), 1 + nb0 + l + 1)
                act.activation(m_xsT[0][:, 0:4, :], bank(0).rearrange("p (k n) -> p k n", k=4), ACT.Copy)\
                    .then_inc(sem("m_ta"), 1)
                with act.Fori(0, NBL[l] // 2) as i:
                    for p in range(2):
                        with act.If(2 * i + p < count):
                            act.wait_ge(sem("m_w1"), nb0 + 2 * i + (p + 3))
                            act.wait_ge(sem("m_h"), 1 + nb0 + 2 * i + p)
                            act.activation(m_sg, bank(2), ACT.Silu).then_inc(sem("m_sg"), 1)
                            act.wait_ge(sem("m_t"), 1 + nb0 + l + 2 * i + (p + 2))
                            act.activation(m_xsT[1 - p][:, 0:4, :], bank(0).rearrange("p (k n) -> p k n", k=4),
                                           ACT.Copy).then_inc(sem("m_ta"), 1)
                            act.wait_ge(sem("m_y"), nb0 + 2 * i + (p + 1))
                            act.wait_ge(sem("m_free"), nb0 + 2 * i + (p + 1))
                            act.activation(m_y[p][:, 0:CW], bank(5), ACT.Copy).then_inc(sem("m_ya"), 1)
                for i_ in range(nt + 1):
                    if i_ < nt:
                        act.wait_ge(sem(f"cg{tiles[i_]}"), 16 * (l + 1))
                        y0 = c_y[tiles[i_]][:, 0, :]
                        act.activation(y0, y0, ACT.Copy, scale=g_gate[0][:, i_:i_ + 1]).then_inc(sem("y0_gated"), 1)
                    if i_ >= 1:
                        row_root(2 * l + 1, i_ - 1)

        @block.tensor
        def _(pe):
            pe.wait_ge(sem("const_in"), 32)
            pe.wait_ge(sem("c_act"), 1)
            cT = mem3(SMALL + V_ST + 40, KD, 2)
            with pe.Fori(0, 8) as i:
                for s in range(3):
                    pe.wait_ge(sem(f"st_w{s}"), 16 * i + 16)
                    pe.wait_ge(sem("ada_free"), 3 * i + (s + 1))
                    for k in range(KD):
                        m = pe.matmul(bank(s)[0:2], cT[:, k, :], slot_cols(s)[:, k, :],
                                      start=(k == 0), stop=(k == KD - 1))
                    m.then_inc(sem("ada_mm"), 1)

            def transposes(r, xn):
                pe.wait_ge(sem("rms_xn"), past("rms_xn", r) + TX)
                for k in range(KD):
                    if k >= 2:
                        pe.wait_ge(sem("rms_hT"), past("rms_hT", r) + k - 1)
                    for t in range(TX):
                        m = pe.transpose(bank(6 + k % 2, P, t * P), xn[:, t, k * P:(k + 1) * P], ident)
                    m.then_inc(sem("rms_tp"), 1)

            transposes(0, c_xn)
            pe.wait_ge(sem("rms_hT"), past("rms_hT", 0) + KD)
            pe.wait_ge(sem("ada_free"), 27)
            with pe.Fori(0, 4) as i:
                for s in range(2):
                    pe.wait_ge(sem(f"cv_w{s}"), 48 * i + 48)
                    for c in range(2):
                        f1 = 4 * i + (2 * s + c + 1)
                        pe.wait_ge(sem("cv_act_free"), f1)
                        pe.wait_ge(sem("cv_dve_free"), f1)
                        for role, b, name in ((1, 2, "cv_b"), (0, 0, "cv_a"), (2, 4, "cv_z")):
                            w = mem3(RING + 6144 * s + 2048 * role, KD, 256)
                            for k in range(KD):
                                m = pe.matmul(bank(b + c), w[:, k, c * P:(c + 1) * P], c_hT[:, k, :],
                                              start=(k == 0), stop=(k == KD - 1))
                            m.then_inc(sem(name), 1)
            pe.wait_ge(sem("ln_sum"), 1)
            pe.matmul(bank(6), c_ones, c_sum, start=True, stop=True).then_inc(sem("ln_mm"), 1)
            for k in range(KI):
                pe.wait_ge(sem("ln_sq"), k + 1)
                pe.matmul(bank(7), c_ones, c_tmp[k % 2], start=(k == 0), stop=(k == KI - 1))\
                    .then_inc(sem("ln_sqadd"), 1)

            def out_product(r, base, y, ready):
                for k in range(KI):
                    ready(k)
                    if k % 4 == 0:
                        n = base + k // 4
                        pe.wait_ge(sem(f"st_w{n % 3}"), 16 * (n // 3 + 9))
                    for t in range(TX):
                        for hf in range(2):
                            m = pe.matmul(bank(2 * t + hf), mem(y + S * k + P * t, P),
                                          slot_rows(n)[:, k % 4, hf * CW:(hf + 1) * CW],
                                          start=(k == 0), stop=(k == KI - 1))
                            if k == KI - 1:
                                m.then_inc(sem("op_mm"), 1)
                            elif k % 4 == 3 and (t, hf) == (TX - 1, 1):
                                m.then_inc(sem("op_chunk"), 1)

            pe.wait_ge(sem("cv_act_free"), KI + 2)
            pe.wait_ge(sem("ln_ve"), 1)
            out_product(0, 0, c_c, lambda k: pe.wait_ge(sem("y_ready"), k + 1))
            transposes(1, r_xn)
            pe.wait_ge(sem("rms_hT"), past("rms_hT", 1) + KD)
            for n in range(12):
                pe.wait_ge(sem(f"st_w{(S_RIN + n) % 3}"), 16 * ((S_RIN + n) // 3 + 9))
                w = slot_cols(S_RIN + n)
                if 2 <= n < 6:
                    pe.wait_ge(sem("ri_dve"), 4 * (n - 1))
                elif n >= 6:
                    pe.wait_ge(sem("ri_act"), 4 * (n - 5))
                for j in range(4):
                    for k in range(KD):
                        l_, r_ = w[:, k, j * P:(j + 1) * P], c_hT[:, k, :]
                        if 4 <= n < 8:
                            l_, r_ = c_hT[:, k, j * P:(j + 1) * P], w[:, k, :]
                        m = pe.matmul(bank(4 * (n % 2) + j), l_, r_, start=(k == 0), stop=(k == KD - 1))
                    m.then_inc(sem("ri_mm"), 1)

            def r_scores(h):
                for j in range(TX):
                    n = TX * h + j
                    if n >= 2:
                        pe.wait_ge(sem("ra_s"), n - 1)
                    for dt in range(2):
                        m = pe.matmul(bank(j % 2, S - P * j), mem(r_k + S * (2 * h + dt) + P * j, P),
                                      mem(r_q + S * (2 * h + dt) + P * j, S - P * j),
                                      start=(dt == 0), stop=(dt == 1))
                    m.then_inc(sem("ra_sc"), 1)

            def r_values(h):
                for i in range(TX):
                    pe.wait_ge(sem("ra_s"), TX * h + i + 1)
                    if h >= 1:
                        pe.wait_ge(sem("ra_on"), TX * h)
                    for j in range(i + 1):
                        m = pe.matmul(bank(4 + i), r_s[j][:, P * (i - j):P * (i - j + 1)],
                                      r_v[:, j, h * RV:(h + 1) * RV], start=(j == 0), stop=(j == i))
                    m.then_inc(sem("ra_o"), 1)

            def r_turn(h):
                for t in range(TX):
                    n = TX * h + t
                    pe.wait_ge(sem("ra_on"), n + 1)
                    if n >= 2:
                        pe.wait_ge(sem("ra_y"), n - 1)
                    for c in range(RV // P):
                        m = pe.transpose(bank(2 + t % 2, P, c * P), r_on[:, t, c * P:(c + 1) * P], ident)
                    m.then_inc(sem("ra_t"), 1)

            pe.wait_ge(sem("ri_act"), 32)
            pe.wait_ge(sem("ri_dve"), 16)
            r_scores(0)
            r_values(0)
            for h in range(1, RH):
                r_scores(h)
                r_turn(h - 1)
                r_values(h)
            r_turn(RH - 1)
            pe.wait_ge(sem("ra_y"), RH * TX)
            out_product(1, S_ROUT, r_g, lambda k: None)
            if stop == 1:
                return

            def mod_transposes(q, i_):
                t, n = mod_order(q)[i_], 4 if q % 2 == 0 else 2
                pe.wait_ge(sem("hx_in"), past("hx_in", q) + (max(i_, 2) if q == 2 else i_) + 1)
                if i_ >= n:
                    pe.wait_ge(sem("hx_Ta"), past("hx_Ta", q) + i_ - n + 1)
                    pe.wait_ge(sem("hx_Td"), past("hx_Td", q) + i_ - n + 1)
                for k in range(KD):
                    m = pe.transpose(bank(mod_bank(q, i_) + k // 4, P, (k % 4) * P), b_hx[:, t, k * P:(k + 1) * P], ident)
                m.then_inc(sem("hx_t"), 1)

            for l in range(LAYERS):
                tiles, outs, units = full(l), in_outputs(l), att_units(l)
                nt, base = len(tiles), S_B2[l]
                for i_ in range(T):
                    mod_transposes(2 * l, i_)
                pe.wait_ge(sem("hx_Ta"), past("hx_Ta", 2 * l) + T)
                pe.wait_ge(sem("hx_Td"), past("hx_Td", 2 * l) + T)
                for n, (c, kind, w, who) in enumerate(outs):
                    if n == 0 or outs[n - 1][0] != c:
                        g = base + c
                        pe.wait_ge(sem(f"st_w{g % 3}"), 16 * (g // 3 + 9))
                        wc = slot_cols(g)
                    if n >= 8:
                        who8 = outs[n - 8][3]
                        pe.wait_ge(sem(f"in_{who8}"), past(f"in_{who8}", l) + taken(outs, n - 8, who8))
                    for k in range(KD):
                        if kind in ("q", "g"):
                            o, l_, r_ = bank(n % 8), b_hxT[:, k, w * P:(w + 1) * P], wc[:, k, :]
                        elif kind == "kv":
                            o, l_, r_ = bank(n % 8, 256), b_hxT[:, k, w * P:(w + 1) * P], wc[:, k, 0:256]
                        else:
                            f, part = w
                            t0, tn, _ = RANGE[part]
                            col = {"cb": 256, "cc": 0, "cx": 256}[kind] + f * P
                            o, l_, r_ = bank(n % 8, tn), wc[:, k, col:col + P], b_hxT[:, k, t0:t0 + tn]
                        m = pe.matmul(o, l_, r_, start=(k == 0), stop=(k == KD - 1))
                    m.then_inc(sem("in_mm"), 1)
                pe.wait_ge(sem("in_dve"), past("in_dve", l) + taken(outs, len(outs), "dve"))
                pe.wait_ge(sem("in_act"), past("in_act", l) + taken(outs, len(outs), "act"))
                for t in range(T):
                    if t in tiles:
                        if t >= 1:
                            pe.wait_ge(sem("qT"), past("qT", l) + t)
                        for j in range(4):
                            m = pe.transpose(bank(6, P, j * P), b_q[:, t, j * P:(j + 1) * P], ident)
                        m.then_inc(sem("qt"), 1)
                    if t >= 1:
                        pe.wait_ge(sem("kT"), past("kT", l) + t)
                    for j in range(KVH):
                        m = pe.transpose(bank(7, P, j * P), b_k[:, t, j * P:(j + 1) * P], ident)
                    m.then_inc(sem("kt"), 1)
                pe.wait_ge(sem("ws"), past("ws", l) + 16)
                for i_, t in enumerate(tiles):
                    pe.wait_ge(sem("gv"), past("gv", l) + i_ + 1)
                    if i_ >= 2:
                        pe.wait_ge(sem("gm_y"), past("gm_y", l) + i_ - 1)
                    for g in range(4):
                        m = pe.matmul(bank(t % 2, 64, 64 * g), b_wsT[:, g, :], b_g[:, t, 256 + 64 * g:320 + 64 * g],
                                      start=True, stop=True)
                    m.then_inc(sem("gm_mm"), 1)
                pe.wait_ge(sem("gm_y"), past("gm_y", l) + nt)
                for t in tiles:
                    for f in range(2):
                        dst = bank(2 + f, P, t * P) if t < TX else bank(4 + f, P, (t - TX) * P)
                        m = pe.transpose(dst, b_g[:, t, 256 + f * P:256 + (f + 1) * P], ident)
                m.then_inc(sem("gm_t"), 1)
                pe.wait_ge(sem("gmT"), past("gmT", l) + (2 if l else 4))
                pe.wait_ge(sem("qT"), past("qT", l) + nt)
                pe.wait_ge(sem("kT"), past("kT", l) + T)

                def scores(u):
                    n, lo, hi, kv = units[u]
                    L = P * (hi - lo + 1)
                    for hh in range(4):
                        h, x = 4 * kv + hh, 4 * u + hh
                        part = slice(HD * (h % 2), HD * (h % 2) + HD)
                        if x >= 2:
                            pu, ph = (x - 2) // 4, (x - 2) % 4
                            pe.wait_ge(sem("at_c"), past("at_c", l) + x - 1)
                            pe.wait_ge(sem("at_l"), past("at_l", l) + local_done(units, pu, ph))
                        q = b_qT[part, h // 2, n * P:(n + 1) * P]
                        o = 1024 * (hh % 2) + 512
                        if L:
                            pe.matmul(psum[:, o - L:o], q, b_kT[part, kv, lo * P:(hi + 1) * P], start=True, stop=True)
                        pe.matmul(psum[:, o:o + C], q, b_kT[part, kv, S:S + C], start=True, stop=True)\
                            .then_inc(sem("at_s"), 1)

                def turn_and_weigh(u):
                    n, lo, hi, kv = units[u]
                    keys = list(range(lo, hi + 1)) + list(range(TX, T))
                    pe.wait_ge(sem("at_p"), past("at_p", l) + u + 1)
                    for c in range(len(keys)):
                        last = (c - 2) if c >= 2 else None
                        if last is not None:
                            pe.wait_ge(sem(f"at_t{'ad'[c % 2]}"), past(f"at_t{'ad'[c % 2]}", l) + at_half_before(units, u, c % 2) + last // 2 + 1)
                        else:
                            pe.wait_ge(sem(f"at_t{'ad'[c % 2]}"), past(f"at_t{'ad'[c % 2]}", l) + at_half_before(units, u, c % 2))
                        for hh in range(4):
                            m = pe.transpose(bank(4 + c % 2, P, hh * P), b_sb[u % 2][:, hh, c * P:(c + 1) * P], ident)
                        m.then_inc(sem("at_t"), 1)
                    if u >= 2:
                        pe.wait_ge(sem("at_o"), past("at_o", l) + 2 * (u - 1))
                    for c, t in enumerate(keys):
                        pe.wait_ge(sem(f"at_t{'ad'[c % 2]}"), past(f"at_t{'ad'[c % 2]}", l) + at_half_before(units, u, c % 2) + c // 2 + 1)
                        m = pe.matmul(bank(6 + u % 2)[0:HD], b_v[:, t, HD * kv:HD * kv + HD], b_pT[:, c, :],
                                      start=(c == 0), stop=(c == len(keys) - 1))
                    m.then_inc(sem("at_pv"), 1)

                scores(0)
                for u in range(len(units)):
                    if u + 1 < len(units):
                        scores(u + 1)
                    turn_and_weigh(u)
                pe.wait_ge(sem("at_o"), past("at_o", l) + 2 * len(units))
                pe.wait_ge(sem("cv_y"), past("cv_y", l) + 2 * (2 - l))
                for n in range(base + 4, base + 6):
                    pe.wait_ge(sem(f"st_w{n % 3}"), 16 * (n // 3 + 9))
                for t in tiles:
                    if t >= 4:
                        pe.wait_ge(sem("ob_x"), past("ob_x", l) + 2 * (t - 3))
                    for hf in range(2):
                        for k in range(KD):
                            y = b_att[:, k] if k < 4 else b_cv[:, k - 4] if k < 6 else b_gmT[:, k - 6]
                            m = pe.matmul(bank(2 * (t % 4) + hf), y[:, t * P:(t + 1) * P],
                                          slot_rows(base + 4 + k // 4)[:, k % 4, hf * CW:(hf + 1) * CW],
                                          start=(k == 0), stop=(k == KD - 1))
                        m.then_inc(sem("ob_mm"), 1)
                if l == 0:
                    for j in ("m_w1", "m_w3", "m_w2"):
                        pe.sem_inc(sem(j), 2)
                    for j in ("m_ht", "m_t"):
                        pe.sem_inc(sem(j), 1)
                pe.wait_ge(sem("ob_x"), past("ob_x", l) + 2 * nt)
                pe.wait_ge(sem("wr"), past("wr", l) + 32)
                for i_ in range(nt + 1):
                    if i_ < nt:
                        mod_transposes(2 * l + 1, i_)
                    if i_ >= 1:
                        t = i_ - 1
                        pe.wait_ge(sem("hx_Ta"), past("hx_Ta", 2 * l + 1) + i_)
                        pe.wait_ge(sem("hx_Td"), past("hx_Td", 2 * l + 1) + i_)
                        for k in range(KD):
                            m = pe.matmul(bank(4, NG + E, (NG + E) * t), b_hxT[:, k, t * P:(t + 1) * P],
                                          b_wr[:, k, :], start=(k == 0), stop=(k == KD - 1))
                        m.then_inc(sem("lg_mm"), 1)
                pe.wait_ge(sem("rt_M"), past("rt_M", l) + 1)
                pe.wait_ge(sem("tok0"), past("tok0", l) + 16)
                M, before = mem(g_a[4], E * nt), mem(g_a[5], E * (nt + 1))
                pe.matmul(bank(5, E * nt), tri, M, start=True, stop=False)
                pe.matmul(bank(5, E * nt), g_ones, before[:, 0:E * nt], start=False, stop=True)
                pe.matmul(bank(5, E, E * nt), g_ones, before[:, E * nt:E * nt + E], start=True, stop=True)\
                    .then_inc(sem("rank"), 1)
                pe.wait_ge(sem("idx"), past("idx", l) + 1)
                NR = NBL[l] + 2
                for o in range(2):
                    m = pe.transpose(bank(6, NR, NR * o), g_rowf[0:NR, :, o], ident[0:NR, 0:NR])
                m.then_inc(sem("rank"), 1)
                pe.wait_ge(sem("meta"), past("meta", l) + 1)
                count = pe.value_load(g_n[l][0:1, 0:1], min_val=2, max_val=NBL[l])
                nb0, rows0 = done_before(pe, l)

                def rows_turned(p, half):
                    for k in range(4 * half, 4 * half + 4):
                        m = pe.transpose(bank(half, P, (k % 4) * P), m_xs[p][:, k * P:(k + 1) * P], ident)
                    if half:
                        m.then_inc(sem("m_t"), 1)

                pe.wait_ge(sem("m_g0"), rows0[0] + (16 * l + 16))
                rows_turned(0, 0)
                rows_turned(0, 1)
                with pe.Fori(0, NBL[l] // 2) as i:
                    for p in range(2):
                        with pe.If(2 * i + p < count):
                            pe.wait_ge(sem("m_ta"), nb0 + l + 2 * i + (p + 1))
                            pe.wait_ge(sem("m_td"), nb0 + l + 2 * i + (p + 1))
                            for j, (b, name) in enumerate(((2, "m_w1"), (3, "m_w3"))):
                                pe.wait_ge(sem(f"m_load{3 * p + j}"), rows0[p] + 16 * i + 16)
                                pe.wait_ge(sem("m_h"), 1 + nb0 + 2 * i + p)
                                w = mem3(RING + CHUNK * (3 * p + j), KD, DE)
                                for k in range(KD):
                                    m = pe.matmul(bank(b), m_xsT[p][:, k, :], w[:, k, :],
                                                  start=(k == 0), stop=(k == KD - 1))
                                m.then_inc(sem(name), 1)
                            pe.wait_ge(sem(f"m_g{1 - p}"), rows0[1 - p] + 16 * i + (16 * l + 16 * p + 16))
                            rows_turned(1 - p, 0)
                            pe.wait_ge(sem("m_h"), 1 + nb0 + 2 * i + (p + 1))
                            for k in range(KE):
                                m = pe.transpose(bank(4, P, k * P), m_h[:, k * P:(k + 1) * P], ident)
                            m.then_inc(sem("m_ht"), 1)
                            rows_turned(1 - p, 1)
                            pe.wait_ge(sem(f"m_load{3 * p + 2}"), rows0[p] + 16 * i + 16)
                            pe.wait_ge(sem("m_ya"), 1 + nb0 + 2 * i + p)
                            pe.wait_ge(sem("m_yd"), 1 + nb0 + 2 * i + p)
                            pe.wait_ge(sem("m_hT"), nb0 + 2 * i + (p + 1))
                            w = mem3(RING + CHUNK * (3 * p + 2), KE, D)
                            for hf in range(2):
                                for k in range(KE):
                                    m = pe.matmul(bank(5 + hf), m_hT[:, k, :], w[:, k, hf * CW:(hf + 1) * CW],
                                                  start=(k == 0), stop=(k == KE - 1))
                                m.then_inc(sem("m_y" if hf == 0 else "m_w2"), 1)

        @block.vector
        def _(dve):
            link = chain(dve, "dve_chain")
            for name in ("m_h", "m_yd"):
                dve.sem_inc(sem(name), 1)

            def rstd(r):
                dve.wait_ge(sem("rms_ss"), past("rms_ss", r) + 1)
                dve.tensor_scalar(stats[:, 0:4], stats[:, 0:4], 1.0 / D, EPS, ALU.mult, ALU.add)\
                    .then_inc(sem("rms_ms"), 1)
                dve.wait_ge(sem("rms_sd"), past("rms_sd", r) + 1)
                link(dve.reciprocal(stats[:, 12:16], stats[:, 8:12]))

            def normalise(r, xn):
                rstd(r)
                for t in range(TX):
                    dve.tensor_scalar(xn[:, t, :], xr[:, t, :], stats[:, 12 + t:13 + t], None, ALU.mult)\
                        .then_inc(sem("rms_xn"), 1)

            normalise(0, c_xn)
            dve.sem_inc(sem("ada_free"), 3)
            dve.wait_ge(sem("x_in"), 16 * (LAYERS + TX))
            def ada_row(l, i, s, first=False):
                dve.wait_ge(sem("ada_mm"), 3 * i + (12 * l + s + 1))
                if not first:
                    dve.wait_ge(sem(f"ada_out{s}"), 16 * i + 64 * l)
                dve.tensor_tensor(a_row[s], bank(s)[0:2],
                                  arena[0:2, bass.ds(i * (3 * CW) + (W0 + 6 * D * l + s * CW), CW)],
                                  ALU.add).then_inc(sem("ada_free"), 1)

            for s in range(3):
                ada_row(0, 0, s, first=True)
            for l in range(LAYERS):
                with dve.Fori(1 - l, 4) as i:
                    for s in range(3):
                        ada_row(l, i, s)
            for p in range(2):
                link(dve.memset(c_up[p][:, 0:TAPS - 1], 0.0))
            dve.sem_inc(sem("cv_dve_free"), 2)
            vw = small[:, V_CW:V_CW + 512]
            PER = TAPS + 2
            dve.wait_ge(sem("ada_saved"), 1)
            with dve.Fori(0, KI // 2) as i:
                for p in range(2):
                    base = (2 * PER) * i + p * PER
                    tap = sem("cv_tap")
                    dve.wait_ge(sem("cv_a"), 2 * i + (p + 1))
                    dve.wait_ge(sem("cv_sg"), 2 * i + (p + 1))
                    dve.tensor_tensor(c_up[p][:, TAPS - 1:TAPS - 1 + S], bank(p), c_sg[p], ALU.mult)\
                        .then_inc(sem("cv_dve_free"), 1)
                    dve.tensor_copy(c_wb[p], arena[:, bass.ds(i * 64 + (SMALL + V_CW + 32 * p), 32)])\
                        .then_inc(tap, 1)
                    dve.wait_ge(sem("cv_dve_free"), 2 * i + (p + 3))
                    dve.wait_ge(tap, base + 1)
                    w = c_wb[p]
                    for j in range(TAPS):
                        u, acc = c_up[p][:, j:j + S], c_acc[p][j % 2]
                        if j >= 2:
                            dve.wait_ge(tap, base + j)
                        if j == 0:
                            ins = dve.tensor_scalar(acc, u, w[:, 0:1], w[:, TAPS:TAPS + 1], ALU.mult, ALU.add)
                        elif j == 1:
                            ins = dve.tensor_scalar(acc, u, w[:, 1:2], None, ALU.mult)
                        else:
                            ins = dve.scalar_tensor_tensor(out=acc, in0=u, scalar=w[:, j:j + 1], in1=acc,
                                                           op0=ALU.mult, op1=ALU.add)
                        ins.then_inc(tap, 1)
                    dve.wait_ge(tap, base + (TAPS + 1))
                    dve.tensor_tensor(arena[:, bass.ds(i * 1024 + (c_c + 512 * p), S)], c_acc[p][0], c_acc[p][1],
                                      ALU.add).then_inc(sem("cv_c"), 1)
                    dve.sem_inc(tap, 1)
            dve.wait_ge(sem("ln_act"), 1)
            with dve.Fori(0, KI) as i:
                cf = arena[:, bass.ds(i * S + c_c, S)]
                dve.tensor_tensor(cf, cf, c_mean, ALU.subtract).then_inc(sem("ln_d"), 1)
            dve.wait_ge(sem("ln_sqadd"), KI + 2)
            dve.tensor_scalar(c_sq, bank(7), EPS, None, ALU.add).then_inc(sem("ln_ve"), 1)
            dve.wait_ge(sem("ln_act"), 2)
            link(dve.reciprocal(c_rstd, c_rstd))
            with dve.Fori(0, KI // 2) as i:
                for p in range(2):
                    dve.wait_ge(sem("ln_s_tok"), 2 * i + (p + 1))
                    dve.tensor_tensor(c_tmp[p], arena[:, bass.ds(i * 1024 + (c_c + 512 * p), S)], c_rstd,
                                      ALU.mult).then_inc(sem("ln_n"), 1)

            def residual(r):
                for t in range(TX):
                    for hf in range(2):
                        dve.wait_ge(sem("op_mm"), past("op_mm", r) + 2 * t + hf + 1)
                        xh = xr[:, t, hf * CW:(hf + 1) * CW]
                        dve.tensor_tensor(xh, xh, bank(2 * t + hf), ALU.add).then_inc(sem("op_x"), 1)

            residual(0)
            dve.wait_ge(sem("op_x"), past("op_x", 0) + 8)
            normalise(1, r_xn)
            dve.wait_ge(sem("pos_in"), 32)
            C1, C2 = 6.28125, 1.9340515136718750e-3
            C3 = float(2 * np.pi - C1 - C2)
            PI_IN = 3.1415925
            link(dve.tensor_copy(r_posf, r_pos.bitcast(I32)))
            link(dve.tensor_scalar(r_ang, r_posf, mem(TAB + T_FREQ, 1), None, ALU.mult))
            for dst, quarter in ((r_cos, 0.25), (r_sin, 0.0)):
                n, ni = r_n[0], r_n[1].bitcast(I32)
                link(dve.tensor_scalar(n, r_ang, float(0.5 / np.pi), quarter, ALU.mult, ALU.add))
                link(dve.tensor_copy(ni, n))
                link(dve.tensor_copy(n, ni))
                link(dve.scalar_tensor_tensor(out=dst, in0=n, scalar=-C1, in1=r_ang, op0=ALU.mult, op1=ALU.add))
                link(dve.scalar_tensor_tensor(out=dst, in0=n, scalar=-C2, in1=dst, op0=ALU.mult, op1=ALU.add))
                link(dve.scalar_tensor_tensor(out=dst, in0=n, scalar=-C3, in1=dst, op0=ALU.mult, op1=ALU.add))
                link(dve.tensor_scalar(dst, dst, float(2 * np.pi * quarter), None, ALU.add))
                link(dve.tensor_scalar(dst, dst, PI_IN, -PI_IN, ALU.min, ALU.max))
            dve.sem_inc(sem("rot_arg"), 1)
            dve.wait_ge(sem("rot"), 2)
            for n in range(4):
                for j in range(2):
                    dve.wait_ge(sem("ri_mm"), 4 * n + 2 * j + 2)
                    b1, b2 = bank(4 * (n % 2) + 2 * j), bank(4 * (n % 2) + 2 * j + 1)
                    o = (r_q if n < 2 else r_k) + S * (4 * (n % 2) + 2 * j)
                    o1, o2 = mem(o, S), mem(o + S, S)
                    dve.tensor_tensor(o1, b1, r_cos, ALU.mult).then_inc(sem("rope"), 1)
                    link(dve.tensor_tensor(r_t[0], b2, r_sin, ALU.mult))
                    dve.wait_ge(sem("rope"), 2 * (2 * n + j) + 1)
                    link(dve.tensor_tensor(o1, o1, r_t[0], ALU.subtract))
                    link(dve.tensor_tensor(o2, b1, r_sin, ALU.mult))
                    dve.tensor_tensor(r_t[1], b2, r_cos, ALU.mult).then_inc(sem("rope"), 1)
                    dve.wait_ge(sem("rope"), 2 * (2 * n + j) + 2)
                    dve.tensor_tensor(o2, o2, r_t[1], ALU.add).then_inc(sem("ri_dve"), 2)

            dve.wait_ge(sem("pos_in"), 32)

            def r_decayed(h):
                for j in range(TX):
                    n = TX * h + j
                    dve.wait_ge(sem("ra_sc"), n + 1)
                    if h >= 1 and j == 0:
                        dve.wait_ge(sem("ra_o"), TX * h)
                    dve.tensor_tensor(r_s[j], bank(j % 2, S - P * j), r_decay[:, h, 0:S - P * j], ALU.mult)\
                        .then_inc(sem("ra_s"), 1)

            def r_norm(h):
                dve.wait_ge(sem("ra_ss"), h + 1)
                dve.tensor_scalar(stats[:, 16:20], stats[:, 16:20], 1.0 / RV, EPS, ALU.mult, ALU.add)\
                    .then_inc(sem("ra_ms"), 1)
                dve.wait_ge(sem("ra_sd"), h + 1)
                link(dve.reciprocal(stats[:, 20:24], stats[:, 24:28]))
                if h >= 1:
                    dve.wait_ge(sem("ra_t"), TX * h)
                for t in range(TX):
                    dve.tensor_scalar(r_on[:, t, :], bank(4 + t), stats[:, 20 + t:21 + t], None, ALU.mult)\
                        .then_inc(sem("ra_on"), 1)

            def r_gate(h):
                for t in range(TX):
                    dve.wait_ge(sem("ra_t"), TX * h + t + 1)
                    g = mem3(r_g + 4 * S * h, 4, S)[:, :, t * P:(t + 1) * P]
                    dve.tensor_tensor(g, bank(2 + t % 2).rearrange("p (c n) -> p c n", c=4), g, ALU.mult)\
                        .then_inc(sem("ra_y"), 1)

            r_decayed(0)
            r_norm(0)
            for h in range(1, RH):
                r_decayed(h)
                r_gate(h - 1)
                r_norm(h)
            r_gate(RH - 1)
            residual(1)
            rstd(2)
            dve.wait_ge(sem("fg_in"), 16)
            dve.wait_ge(sem("op_x"), past("op_x", 1) + 8)
            for t in range(TX):
                dve.scalar_tensor_tensor(out=xr[:, t, :], in0=xr[:, t, :], scalar=stats[:, 12 + t:13 + t],
                                         in1=f_g, op0=ALU.mult, op1=ALU.mult).then_inc(sem("fin_x"), 1)
            if stop == 1:
                return

            def finish_rows(q, tiles, first, mod_q, sc, free=None):
                nt = len(tiles)

                def stats_of(i_):
                    first(i_, tiles[i_])
                    for hf in range(2):
                        link(dve.bn_stats(stats[:, 100 + 12 * i_ + 6 * hf:106 + 12 * i_ + 6 * hf],
                                          xr[:, tiles[i_], hf * CW:(hf + 1) * CW]))
                    link(dve.bn_aggr(stats[:, 172 + 2 * i_:174 + 2 * i_], stats[:, 100 + 12 * i_:112 + 12 * i_]))
                    dve.tensor_scalar(stats[:, 184 + i_:185 + i_], stats[:, 173 + 2 * i_:174 + 2 * i_], LN_EPS, None,
                                      ALU.add).then_inc(sem("row_ve"), 1)

                def norm(i_):
                    x_t = xr[:, tiles[i_], :]
                    dve.wait_ge(sem("row_sd"), past_rows(q) + i_ + 1)
                    link(dve.reciprocal(stats[:, 196 + i_:197 + i_], stats[:, 190 + i_:191 + i_]))
                    link(dve.tensor_scalar(x_t, x_t, stats[:, 172 + 2 * i_:173 + 2 * i_],
                                           stats[:, 196 + i_:197 + i_], ALU.subtract, ALU.mult))
                    dve.tensor_tensor(x_t, x_t, b_ln[0], ALU.mult).then_inc(sem("row_n"), 1)

                def mod_next(i_):
                    dve.wait_ge(sem("row_x"), past_rows(q) + i_ + 1)
                    if mod_q % 2 == 0:
                        dve.wait_ge(sem("mod_in"), past("mod_in", mod_q // 2) + 64)
                    if free and tiles[i_] >= TX:
                        free()
                    modulated(tiles[i_], sc)

                dve.wait_ge(sem("row_w"), 32 * (q + 1))
                for i_ in range(nt - 1):
                    stats_of(i_)
                    if i_ >= 1:
                        norm(i_ - 1)
                    if i_ >= 2 and mod_q is not None:
                        mod_next(i_ - 2)
                stats_of(nt - 1)
                norm(nt - 2)
                if mod_q is None:
                    norm(nt - 1)
                    return
                mod_next(nt - 3)
                mod_copy(mod_q, 0)
                norm(nt - 1)
                mod_copy(mod_q, 1)
                mod_next(nt - 2)
                mod_next(nt - 1)
                for i_ in range(2, nt):
                    mod_copy(mod_q, i_)

            def modulated(t, sc):
                dve.scalar_tensor_tensor(out=b_hx[:, t, :], in0=b_mod[sc[t >= TX]], scalar=1.0, in1=xr[:, t, :],
                                         op0=ALU.add, op1=ALU.mult).then_inc(sem("hx_scaled"), 1)

            def mod_copy(q, i_):
                t = mod_order(q)[i_]
                dve.wait_ge(sem("hx_t"), past("hx_t", q) + i_ + 1)
                dve.tensor_copy(b_hxT[:, 4:8, t * P:(t + 1) * P],
                                bank(mod_bank(q, i_) + 1).rearrange("p (k n) -> p k n", k=4)).then_inc(sem("hx_Td"), 1)

            dve.wait_ge(sem("rows_in"), 64)
            dve.wait_ge(sem("mod_in"), 64)
            dve.wait_ge(sem("ctx_in"), 16 * TC)
            for t in mod_order(0):
                if t < TX:
                    dve.wait_ge(sem("fin_x"), t + 1)
                modulated(t, (3, 5))
            for i_ in range(T):
                mod_copy(0, i_)
            for l in range(LAYERS):
                tiles, outs, units = full(l), in_outputs(l), att_units(l)
                nt = len(tiles)

                def rotate(dst, src, t, heads):
                    cos, sin = (mem(TAB + T_ROPE + 64 * t + 32 * j, 32).rearrange("p (f d) -> p f d", f=2)
                                .unsqueeze(1).to_broadcast([P, heads, 2, 16]) for j in range(2))
                    def pair(x):
                        v = x.rearrange("p (h f a d) -> p h f a d", f=2, a=2, d=16)
                        return v[:, :, :, 0, :], v[:, :, :, 1, :]
                    (xa, xb), (ya, yb) = pair(src), pair(dst)
                    t0, t1 = (b_t[j][:, 0:32 * heads].rearrange("p (h f d) -> p h f d", f=2, d=16) for j in range(2))
                    link(dve.tensor_tensor(ya, xa, cos, ALU.mult))
                    link(dve.tensor_tensor(t0, xb, sin, ALU.mult))
                    link(dve.tensor_tensor(ya, ya, t0, ALU.subtract))
                    link(dve.tensor_tensor(yb, xb, cos, ALU.mult))
                    link(dve.tensor_tensor(t1, xa, sin, ALU.mult))
                    return dve.tensor_tensor(yb, yb, t1, ALU.add)

                dve.wait_ge(sem("upad"), past("upad", l) + 1)
                for n, (_, kind, w, who) in enumerate(outs):
                    if who != "dve":
                        continue
                    dve.wait_ge(sem("in_mm"), past("in_mm", l) + n + 1)
                    done = sem("in_dve")
                    if kind == "q":
                        if w < TX:
                            rotate(b_q[:, w, :], bank(n % 8), w, AH).then_inc(done, 1)
                        else:
                            dve.tensor_copy(b_q[:, w, :], bank(n % 8)).then_inc(done, 1)
                    elif kind == "kv":
                        link(dve.tensor_copy(b_v[:, w, :], bank(n % 8, P, P)))
                        kd = b_k[:, w, :].rearrange("p (kv two d) -> p kv two d", two=2, d=HD)
                        if w < TX:
                            link(rotate(b_tk, bank(n % 8, P), w, KVH))
                        else:
                            link(dve.tensor_copy(b_tk, bank(n % 8, P)))
                        src = b_tk.rearrange("p (kv d) -> p kv d", d=HD)
                        link(dve.tensor_copy(kd[:, :, 0, :], src))
                        dve.tensor_copy(kd[:, :, 1, :], src).then_inc(done, 1)
                    else:
                        f, part = w
                        t0, tn, place = RANGE[part]
                        u = b_u[:, f, place:place + tn]
                        m = max(i_ for i_, o in enumerate(outs) if o[1] == "cc" and o[2] == w)
                        dve.wait_ge(sem("in_act"), past("in_act", l) + taken(outs, m, "act"))
                        dve.tensor_tensor(u, u, bank(n % 8, tn), ALU.mult).then_inc(done, 1)
                        dve.wait_ge(sem("in_dve"), past("in_dve", l) + taken(outs, n, "dve"))
                        acc = mem(b_acc, tn)
                        cw = [small[:, V_SC + 6 * l + 3 * f + j:V_SC + 6 * l + 3 * f + j + 1] for j in range(3)]
                        src = [b_u[:, f, place - 1 + j:place - 1 + j + tn] for j in range(3)]
                        link(dve.tensor_scalar(acc, src[0], cw[0], None, ALU.mult))
                        for j in (1, 2):
                            link(dve.scalar_tensor_tensor(out=acc, in0=src[j], scalar=cw[j], in1=acc,
                                                          op0=ALU.mult, op1=ALU.add))
                        cv = b_cv[:, f, t0:t0 + tn]
                        dve.tensor_tensor(cv, cv, acc, ALU.mult).then_inc(sem("cv_y"), 1)
                        dve.wait_ge(sem("cv_y"), past("cv_y", l) + f * (2 - l) + part + 1)
                for t in range(T):
                    dve.wait_ge(sem("kt"), past("kt", l) + t + 1)
                    dve.tensor_copy(b_kT[:, :, t * P:(t + 1) * P], bank(7, 256).rearrange("p (j n) -> p j n", j=KVH))\
                        .then_inc(sem("kT"), 1)
                for i_, t in enumerate(tiles):
                    dve.wait_ge(sem("in_act"), past("in_act", l) + taken(outs, len(outs), "act") - nt + i_ + 1)
                    link(dve.bn_stats(stats[:, 100 + 6 * i_:106 + 6 * i_], b_g[:, t, 256:512]))
                    link(dve.bn_aggr(stats[:, 172 + 2 * i_:174 + 2 * i_], stats[:, 100 + 6 * i_:106 + 6 * i_]))
                mv = stats[:, 172:172 + 2 * nt].rearrange("p (t two) -> p t two", two=2)
                dve.tensor_scalar(stats[:, 184:184 + nt], mv[:, :, 1], LN_EPS, None, ALU.add)\
                    .then_inc(sem("gm_ve"), 1)
                dve.wait_ge(sem("gm_sd"), past("gm_sd", l) + 1)
                link(dve.reciprocal(stats[:, 196:196 + nt], stats[:, 190:190 + nt]))
                for i_, t in enumerate(tiles):
                    gv = b_g[:, t, 256:512]
                    dve.tensor_scalar(gv, gv, stats[:, 172 + 2 * i_:173 + 2 * i_], stats[:, 196 + i_:197 + i_],
                                      ALU.subtract, ALU.mult).then_inc(sem("gv"), 1)
                for i_, t in enumerate(tiles):
                    dve.wait_ge(sem("gm_mm"), past("gm_mm", l) + i_ + 1)
                    for g in range(4):
                        ins = dve.scalar_tensor_tensor(
                            out=b_g[:, t, 256 + 64 * g:320 + 64 * g], in0=bank(t % 2, 64, 64 * g),
                            scalar=small[:, V_GB + 4 * l + g:V_GB + 4 * l + g + 1],
                            in1=b_g[:, t, 64 * g:64 * g + 64], op0=ALU.add, op1=ALU.mult)
                    ins.then_inc(sem("gm_y"), 1)

                def local_scores(u):
                    n, lo, hi, kv = units[u]
                    L = P * (hi - lo + 1)
                    sb = b_sb[u % 2]
                    if u == 0:
                        dve.wait_ge(sem("gm_y"), past("gm_y", l) + nt)
                    for hh in range(4):
                        if not L:
                            break
                        dve.wait_ge(sem("at_s"), past("at_s", l) + 4 * u + hh + 1)
                        o = 1024 * (hh % 2) + 512
                        off = TAB + T_BAND + P * (lo - n + 1)
                        dve.scalar_tensor_tensor(out=sb[:, hh, 0:L], in0=psum[:, o - L:o], scalar=SCALE,
                                                 in1=mem(off, L), op0=ALU.mult, op1=ALU.add)\
                            .then_inc(sem("at_l"), 1)

                def maxima(u):
                    n, lo, hi, kv = units[u]
                    W = P * (hi - lo + 1) + C
                    sb = b_sb[u % 2]
                    dve.wait_ge(sem("at_l"), past("at_l", l) + local_done(units, u, 3))
                    dve.wait_ge(sem("at_c"), past("at_c", l) + 4 * u + 4)
                    o = 200 + 32 * (u % 2)
                    mx, nm, sk = (stats[:, o + 4 * j:o + 4 * j + 4] for j in range(3))
                    sink = small[:, V_SINK + AH * l + 4 * kv:V_SINK + AH * l + 4 * kv + 4]
                    link(dve.tensor_reduce(mx, sb[:, :, 0:W], AX.X, ALU.max))
                    link(dve.tensor_tensor(mx, mx, sink, ALU.max))
                    link(dve.tensor_scalar(nm, mx, -1.0, None, ALU.mult))
                    dve.tensor_tensor(sk, sink, mx, ALU.subtract).then_inc(sem("at_m"), 1)

                def weights(u):
                    n, lo, hi, kv = units[u]
                    W = P * (hi - lo + 1) + C
                    dve.wait_ge(sem("at_e"), past("at_e", l) + 5 * u + 5)
                    o = 200 + 32 * (u % 2)
                    rs, esk, rinv = (stats[:, o + 4 * j:o + 4 * j + 4] for j in (3, 4, 5))
                    link(dve.tensor_tensor(rs, rs, esk, ALU.add))
                    link(dve.reciprocal(rinv, rs))
                    for hh in range(4):
                        sb = b_sb[u % 2][:, hh, 0:W]
                        ins = dve.tensor_scalar(sb, sb, rinv[:, hh:hh + 1], None, ALU.mult)
                    ins.then_inc(sem("at_p"), 1)

                def turned(u):
                    n, lo, hi, kv = units[u]
                    for c in range(1, hi - lo + 1 + TC, 2):
                        dve.wait_ge(sem("at_t"), past("at_t", l) + at_t_before(units, u) + c + 1)
                        dve.tensor_copy(b_pT[:, c, :], bank(5)).then_inc(sem("at_td"), 1)

                local_scores(0)
                maxima(0)
                for u in range(len(units)):
                    weights(u)
                    if u + 1 < len(units):
                        local_scores(u + 1)
                    turned(u)
                    if u + 1 < len(units):
                        maxima(u + 1)
                dve.wait_ge(sem("mod_in"), past("mod_in", l) + 64 + 48 * (2 - l))
                dve.wait_ge(sem("at_pv"), past("at_pv", l) + len(units))

                def add_product(i_, t):
                    for hf in range(2):
                        dve.wait_ge(sem("ob_mm"), past("ob_mm", l) + 2 * i_ + hf + 1)
                        cols = slice(hf * CW, (hf + 1) * CW)
                        dve.tensor_tensor(b_tmp[:, cols], bank(2 * (t % 4) + hf), b_mod[3 * (t >= TX)][:, cols],
                                          ALU.mult).then_inc(sem("ob_x"), 1)
                        dve.wait_ge(sem("ob_x"), past("ob_x", l) + 2 * i_ + hf + 1)
                        link(dve.scalar_tensor_tensor(out=xr[:, t, cols], in0=xr[:, t, cols], scalar=ALPHA,
                                                      in1=b_tmp[:, cols], op0=ALU.mult, op1=ALU.add))

                finish_rows(2 * l, tiles, add_product, 2 * l + 1, (1, 4),
                            lambda: dve.wait_ge(sem("ob_mm"), past("ob_mm", l) + 2 * nt))

                def arr(o, *dims):
                    n = int(np.prod(dims))
                    v = mem(o, n)
                    if len(dims) == 2:
                        v = v.rearrange("p (a b) -> p a b", a=dims[0])
                    if len(dims) == 3:
                        v = v.rearrange("p (a b c) -> p a b c", a=dims[0], b=dims[1])
                    return v

                def over(v, *shape):
                    return v.unsqueeze(2).to_broadcast([P, *shape])

                lg = arr(g_lg, nt, NG + E)
                el, oh1, oh2, cand, M = (arr(o, nt, E) for o in g_a[:5])
                before = arr(g_a[5], nt + 1, E)
                ge = arr(g_s, nt, NG)
                ed, gmax, gs, gi, m1, m2, i1, i2, den = (mem(g_s + 24 + 6 * j, 6)[:, 0:nt] for j in range(9))
                goh, gc = arr(g_s + 80, nt, NG), arr(g_s + 104, nt, NG)
                cnt, nb, pst, pend = (mem(g_s + 128 + 32 * j, E) for j in range(4))
                be = mem(g_s + 256, 48)
                iota = mem(TAB + T_EI, E)

                def first_of(dst, idx, vals, top, width):
                    it = iota[:, 0:width].unsqueeze(1).to_broadcast([P, nt, width])
                    link(dve.tensor_tensor(dst, vals, over(top, nt, width), ALU.is_equal))
                    link(dve.scalar_tensor_tensor(out=dst, in0=dst, scalar=-1000.0, in1=it, op0=ALU.mult, op1=ALU.add))
                    link(dve.tensor_reduce(idx, dst, AX.X, ALU.min))
                    link(dve.tensor_tensor(dst, dst, over(idx, nt, width), ALU.is_equal))

                dve.wait_ge(sem("lg_mm"), past("lg_mm", l) + nt)
                rb = mem(SMALL + V_RB + (NG + E) * l, NG + E).unsqueeze(1).to_broadcast([P, nt, NG + E])
                link(dve.tensor_tensor(lg, bank(4, (NG + E) * nt).rearrange("p (t e) -> p t e", t=nt), rb, ALU.add))
                link(dve.tensor_reduce(gmax, lg[:, :, 0:NG], AX.X, ALU.max))
                dve.tensor_tensor(ge, lg[:, :, 0:NG], over(gmax, nt, NG), ALU.subtract).then_inc(sem("rt_dve"), 1)
                first_of(goh, gi, lg[:, :, 0:NG], gmax, NG)
                link(dve.tensor_scalar(gc, goh, -1.0, BIG, ALU.add, ALU.mult))
                for t in range(nt):
                    link(dve.tensor_tensor(el[:, t, :].rearrange("p (g e) -> p g e", g=NG),
                                           lg[:, t, NG:NG + E].rearrange("p (g e) -> p g e", g=NG),
                                           gc[:, t, :].unsqueeze(2).to_broadcast([P, NG, EPG]), ALU.add))
                link(dve.tensor_reduce(m1, el, AX.X, ALU.max))
                first_of(oh1, i1, el, m1, E)
                link(dve.scalar_tensor_tensor(out=el, in0=oh1, scalar=-3 * BIG, in1=el, op0=ALU.mult, op1=ALU.add))
                link(dve.tensor_reduce(m2, el, AX.X, ALU.max))
                first_of(oh2, i2, el, m2, E)
                dve.tensor_tensor(ed, m2, m1, ALU.subtract).then_inc(sem("rt_dve"), 1)
                link(dve.tensor_tensor(M, oh1, oh2, ALU.add))
                link(dve.memset(before[:, 0, :], 0.0))
                for t in range(nt - 1):
                    link(dve.tensor_tensor(before[:, t + 1, :], before[:, t, :], M[:, t, :], ALU.add))
                dve.tensor_tensor(before[:, nt, :], before[:, nt - 1, :], M[:, nt - 1, :], ALU.add)\
                    .then_inc(sem("rt_M"), 1)
                dve.wait_ge(sem("rt_act"), past("rt_act", l) + 1)
                link(dve.tensor_reduce(gs, ge, AX.X, ALU.add))
                dve.wait_ge(sem("rt_act"), past("rt_act", l) + 2)
                link(dve.tensor_scalar(den, ed, 1.0, None, ALU.add))
                link(dve.tensor_tensor(den, den, gs, ALU.mult))
                g0, g1 = (g[:, 0:nt] for g in g_gate)
                link(dve.reciprocal(g0, den))
                link(dve.tensor_tensor(g1, g0, ed, ALU.mult))
                ids = g_ids.rearrange("p (t k) o -> p t k o", k=2)
                for k_ in range(2):
                    link(dve.tensor_copy(ids[:, :, k_, 0], mem(TAB + T_TOK, T)))
                    link(dve.tensor_scalar(ids[:, :, k_, 1], mem(TAB + T_TOK, T), 2.0, float(k_), ALU.mult, ALU.add))
                dve.sem_inc(sem("dest"), 1)
                dve.wait_ge(sem("rank"), past("rank", l) + 1)
                link(dve.tensor_copy(cnt, bank(5, E, E * nt)))
                link(dve.tensor_scalar(nb, cnt, 0.0, None, ALU.is_gt))
                for j in range(1, nt):
                    link(dve.scalar_tensor_tensor(out=nb, in0=cnt, scalar=float(P * j), in1=nb,
                                                  op0=ALU.is_gt, op1=ALU.add))
                link(dve.tensor_tensor(g_prod, g_lower, nb.unsqueeze(1).to_broadcast([P, E, E]), ALU.mult))
                link(dve.tensor_reduce(pst, g_prod, AX.X, ALU.add))
                link(dve.tensor_tensor(pend, pst, nb, ALU.add))
                offs = cand
                link(dve.scalar_tensor_tensor(out=offs, in0=pst.unsqueeze(1).to_broadcast([P, nt, E]),
                                              scalar=float(P), in1=bank(5, E * nt).rearrange("p (t e) -> p t e", t=nt),
                                              op0=ALU.mult, op1=ALU.add))
                for k_, oh in enumerate((oh1, oh2)):
                    link(dve.tensor_tensor(oh, oh, offs, ALU.mult))
                    link(dve.tensor_reduce(i1, oh, AX.X, ALU.add))
                    dve.tensor_copy(g_dest[k_][:, 0:nt], i1).then_inc(sem("dest"), 1)
                    dve.wait_ge(sem("dest"), past("dest", l) + k_ + 2)
                cmp = g_cmp
                link(dve.tensor_tensor(cmp, mem(TAB + T_BI, 48, 1).unsqueeze(2).to_broadcast([1, 48, E]),
                                       pend[0:1].unsqueeze(1).to_broadcast([1, 48, E]), ALU.is_ge))
                link(dve.tensor_reduce(be[0:1], cmp, AX.X, ALU.add))
                link(dve.tensor_scalar(be[0:1], be[0:1], float(E - 1), None, ALU.min))
                link(dve.tensor_copy(g_be[0:1, 0:48], be[0:1]))
                last = pend[0:1, E - 1:E]
                link(dve.tensor_copy(g_n[l][0:1, 0:1], last))
                half = be[0:1, 0:1]
                link(dve.tensor_scalar(half, last, -0.5, 0.5, ALU.add, ALU.mult))
                link(dve.tensor_copy(g_n[l][0:1, 2:3], half))
                link(dve.tensor_copy(half, g_n[l][0:1, 2:3]))
                link(dve.tensor_scalar(be[0:1, 1:2], half, 16.0, None, ALU.mult))
                link(dve.tensor_copy(g_n[l][0:1, 2:3], be[0:1, 1:2]))
                link(dve.tensor_tensor(half, last, half, ALU.subtract))
                link(dve.tensor_scalar(half, half, 16.0, None, ALU.mult))
                link(dve.tensor_copy(g_n[l][0:1, 1:2], half))
                dve.sem_inc(sem("meta"), 1)
                NR = NBL[l] + 2
                dve.wait_ge(sem("tok0"), past("tok0", l) + 32)
                dve.tensor_copy(g_rowf[0:NR], g_rows[0:NR]).then_inc(sem("idx"), 1)
                dve.wait_ge(sem("rank"), past("rank", l) + 2)
                dve.tensor_copy(g_idx[:, :, 0:NR], bank(6, 2 * NR).rearrange("p (o n) -> p o n", o=2)).then_inc(sem("idx"), 1)
                count = dve.value_load(g_n[l][0:1, 0:1], min_val=2, max_val=NBL[l])
                nb0, rows0 = done_before(dve, l)
                dve.wait_ge(sem("m_t"), 1 + nb0 + l + 1)
                dve.tensor_copy(m_xsT[0][:, 4:8, :], bank(1).rearrange("p (k n) -> p k n", k=4))\
                    .then_inc(sem("m_td"), 1)
                with dve.Fori(0, NBL[l] // 2) as i:
                    for p in range(2):
                        with dve.If(2 * i + p < count):
                            dve.wait_ge(sem("m_w3"), nb0 + 2 * i + (p + 3))
                            dve.wait_ge(sem("m_sg"), nb0 + 2 * i + (p + 1))
                            dve.wait_ge(sem("m_ht"), 1 + nb0 + 2 * i + p)
                            dve.tensor_tensor(m_h, m_sg, bank(3), ALU.mult).then_inc(sem("m_h"), 1)
                            dve.wait_ge(sem("m_ht"), 1 + nb0 + 2 * i + (p + 1))
                            dve.tensor_copy(m_hT, bank(4).rearrange("p (k n) -> p k n", k=KE))\
                                .then_inc(sem("m_hT"), 1)
                            dve.wait_ge(sem("m_t"), 1 + nb0 + l + 2 * i + (p + 2))
                            dve.tensor_copy(m_xsT[1 - p][:, 4:8, :], bank(1).rearrange("p (k n) -> p k n", k=4))\
                                .then_inc(sem("m_td"), 1)
                            dve.wait_ge(sem("m_w2"), nb0 + 2 * i + (p + 3))
                            dve.wait_ge(sem("m_free"), nb0 + 2 * i + (p + 1))
                            dve.tensor_copy(m_y[p][:, CW:D], bank(6)).then_inc(sem("m_yd"), 1)
                dve.wait_ge(sem("mod_in"), past("mod_in", l) + 64 + 64 * (2 - l))

                def combine(i_, t):
                    y0, y1 = c_y[t][:, 0, :], c_y[t][:, 1, :]
                    dve.wait_ge(sem(f"cg{t}"), 16 * (l + 1))
                    dve.wait_ge(sem("y0_gated"), T * l + i_ + 1)
                    link(dve.scalar_tensor_tensor(out=y0, in0=y1, scalar=g_gate[1][:, i_:i_ + 1], in1=y0,
                                                  op0=ALU.mult, op1=ALU.add))
                    link(dve.tensor_tensor(y0, y0, b_mod[int(t >= TX)], ALU.mult))
                    link(dve.scalar_tensor_tensor(out=xr[:, t, :], in0=xr[:, t, :], scalar=ALPHA, in1=y0,
                                                  op0=ALU.mult, op1=ALU.add))

                if l + 1 < LAYERS:
                    finish_rows(2 * l + 1, tiles, combine, 2 * l + 2, (3, 5))
                else:
                    finish_rows(2 * l + 1, tiles, combine, None, None)

        @block.gpsimd
        def _(pool):
            link = chain(pool, "pool_chain")
            for l in range(LAYERS):
                with pool.Fori(0, 4) as i:
                    for s in range(3):
                        pool.wait_ge(sem("ada_free"), 3 * i + (12 * l + s + 4))
                        pool.dma_start(mod[l][:, bass.ds(i * (3 * CW) + s * CW, CW)], a_row[s])\
                            .then_inc(sem(f"ada_out{s}"), 16)
            for s in range(3):
                pool.wait_ge(sem(f"ada_out{s}"), 16 * 8)
            link(pool.memset(c_ones, 1.0 / DI))
            link(pool.memset(c_sum, 0.0))
            pool.sem_inc(sem("ada_saved"), 1)
            with pool.Fori(0, KI) as i:
                pool.wait_ge(sem("cv_c"), i + 1)
                pool.tensor_tensor(c_sum, c_sum, arena[:, bass.ds(i * S + c_c, S)], ALU.add)\
                    .then_inc(sem("cv_sum"), 1)
                pool.wait_ge(sem("cv_sum"), i + 1)
            pool.sem_inc(sem("ln_sum"), 1)
            pool.sem_inc(sem("y_ready_tok"), 2)
            pool.sem_inc(sem("ln_s_tok"), 2)
            with pool.Fori(0, KI // 2) as i:
                for p in range(2):
                    pool.wait_ge(sem("ln_s"), 2 * i + (p + 1))
                    pool.sem_inc(sem("ln_s_tok"), 1)
                    pool.tensor_tensor(arena[:, bass.ds(i * 1024 + (c_c + 512 * p), S)], c_tmp2[p],
                                       arena[:, bass.ds(i * 1024 + (c_z + 512 * p), S)], ALU.mult)\
                        .then_inc(sem("y_ready"), 1)
                    pool.wait_ge(sem("y_ready"), 2 * i + (p + 1))
                    pool.sem_inc(sem("y_ready_tok"), 1)
            if stop == 1:
                return

            def add_bias(q, i_, t):
                pool.wait_ge(sem("row_n"), past_rows(q) + i_ + 1)
                pool.tensor_tensor(xr[:, t, :], xr[:, t, :], b_ln[1], ALU.add).then_inc(sem("row_x"), 1)

            def add_shift(q, i_, sh):
                t = mod_order(q)[i_]
                pool.wait_ge(sem("hx_scaled"), past("hx_in", q) + i_ + 1)
                pool.tensor_tensor(b_hx[:, t, :], b_hx[:, t, :], b_mod[sh[t >= TX]], ALU.add)\
                    .then_inc(sem("hx_in"), 1)

            def finish_rows(q, tiles, mod_q, sh):
                pool.wait_ge(sem("row_w"), 32 * (q + 1))
                for i_, t in enumerate(tiles):
                    add_bias(q, i_, t)
                    if i_ >= 1 and mod_q is not None:
                        add_shift(mod_q, i_ - 1, sh)
                if mod_q is not None:
                    add_shift(mod_q, len(tiles) - 1, sh)

            for i_ in range(T):
                add_shift(0, i_, (2, 4))
            for l in range(LAYERS):
                tiles = full(l)
                nt = len(tiles)
                NR = NBL[l] + 2
                pool.memset(b_u, 0.0).then_inc(sem("upad"), 1)
                finish_rows(2 * l, tiles, 2 * l + 1, (2, 5))
                link(pool.memset(g_init[:, :, 0], 0))
                link(pool.memset(g_init[:, :, 1], 4096))
                link(pool.memset(g_ones, 1.0))
                pool.dma_start(slot_tok[l].rearrange("(p n) o -> p n o", n=NR), g_init[:, 0:NR, :])\
                    .then_inc(sem("tok0"), 16)
                pool.wait_ge(sem("tok0"), past("tok0", l) + 16)
                pool.wait_ge(sem("dest"), past("dest", l) + 3)
                for i_ in range(nt):
                    for k in range(2):
                        pool.indirect_dma_start(out=slot_tok[l], in_=g_ids[:, 2 * i_ + k, :],
                                                out_offset=bass.IndirectOffsetOnAxis(g_dest[k][:, i_:i_ + 1], 0),
                                                in_offset=None).then_inc(sem("tok"), 16)
                pool.wait_ge(sem("tok"), past("tok", l) + 32 * nt)
                pool.dma_start(g_rows[0:NR], slot_tok[l].rearrange("(n p) o -> n p o", p=P))\
                    .then_inc(sem("tok0"), 16)
                pool.wait_ge(sem("idx"), past("idx", l) + 2)
                pool.wait_ge(sem("hx2_out"), past("hx2_out", l) + 16 * nt)

                def settled():
                    pool.sem_inc(sem("settled"), 1)

                def gather(p, block):
                    pool.tensor_copy(m_gi[p], g_idx[:, 0, block]).then_inc(sem("m_ib"), 1)

                def fetch(p):
                    settled()
                    pool.indirect_dma_start(out=m_xs[p], in_=moe_in[l], out_offset=None,
                                            in_offset=bass.IndirectOffsetOnAxis(m_gi[p], 0))\
                        .then_inc(sem(f"m_g{p}"), 16)

                pool.wait_ge(sem("meta"), past("meta", l) + 1)
                count = pool.value_load(g_n[l][0:1, 0:1], min_val=2, max_val=NBL[l])
                nb0, rows0 = done_before(pool, l)
                for p in range(2):
                    gather(p, slice(p, p + 1))
                    pool.wait_ge(sem("m_ib"), 2 * nb0 + (2 * l + p + 1))
                    fetch(p)
                with pool.Fori(0, NBL[l] // 2) as i:
                    for p in range(2):
                        with pool.If(2 * i + p < count):
                            pool.wait_ge(sem("m_t"), 1 + nb0 + l + 2 * i + (p + 1))
                            gather(p, bass.ds(2 * i + (p + 2), 1))
                            pool.wait_ge(sem("m_ib"), 2 * nb0 + 4 * i + (2 * l + 2 * p + 3))
                            fetch(p)
                            with pool.If(i > 0):
                                pool.wait_ge(sem(f"m_out{p}"), rows0[p] + 16 * i)
                            pool.sem_inc(sem("m_free"), 1)
                            pool.tensor_copy(m_si[p], g_idx[:, 1, bass.ds(2 * i + p, 1)]).then_inc(sem("m_ib"), 1)
                            pool.wait_ge(sem("m_ib"), 2 * nb0 + 4 * i + (2 * l + 2 * p + 4))
                            pool.wait_ge(sem("m_ya"), 1 + nb0 + 2 * i + (p + 1))
                            pool.wait_ge(sem("m_yd"), 1 + nb0 + 2 * i + (p + 1))
                            settled()
                            pool.indirect_dma_start(out=moe_out[l], in_=m_y[p], in_offset=None,
                                                    out_offset=bass.IndirectOffsetOnAxis(m_si[p], 0),
                                                    bounds_check=2 * nt * P - 1, oob_is_err=False)\
                                .then_inc(sem(f"m_out{p}"), 16)
                rows = [pool.value_load(g_n[l][0:1, 1 + p:2 + p], min_val=16, max_val=16 * NBL[l]) for p in range(2)]
                for p in range(2):
                    pool.wait_ge(sem(f"m_out{p}"), rows0[p] + rows[p])
                    pool.wait_ge(sem(f"m_g{p}"), rows0[p] + rows[p] + (16 * l + 16))
                settled()
                pool.sem_inc(sem("m_done"), 1)
                finish_rows(2 * l + 1, tiles, 2 * l + 2 if l + 1 < LAYERS else None, (2, 4))


def vectors(conv_dw_w, conv_dw_b, conv_ln_g, conv_ln_b, conv_norm, ret_norm, c_2, c_ctx_2, conv_w_2, gm_bs_2):
    def cols(v):
        return np.asarray(v).reshape(-1, P).T

    cw = np.concatenate([np.asarray(conv_dw_w)[0], np.asarray(conv_dw_b)], 0)
    cw = cw.reshape(32, KI, P).transpose(2, 1, 0).reshape(P, 512)
    c = np.stack([np.asarray(c_2)[0], np.asarray(c_ctx_2)]).reshape(2, KD, P).transpose(2, 1, 0).reshape(P, 16)
    sc = np.asarray(conv_w_2).reshape(LAYERS, 3, 2, P).transpose(3, 0, 2, 1).reshape(P, 12)
    gb = np.asarray(gm_bs_2).transpose(2, 0, 1).reshape(P, 8)
    return np.ascontiguousarray(np.concatenate(
        [cw, cols(conv_ln_g[0]), cols(conv_ln_b[0]), cols(conv_norm[0]), cols(ret_norm[0]), c, sc, gb], 1))


def kernel(**inputs):
    import numpy as _np
    import concourse.bacc as _bacc
    from concourse import mybir as _mybir
    from concourse.bass_utils import run_bass_kernel_spmd as _run

    v = {k: _np.asarray(x) for k, x in inputs.items()}
    tab, decay, lower = tables()
    arrays = {
        "x": v["x"][0], "ctx": v["ctx_2"][0], "positions": v["positions"], "tab": tab, "decay": decay,
        "lower": lower, "final_norm": v["final_norm"],
        "vec": vectors(*(v[k] for k in ("conv_dw_w", "conv_dw_b", "conv_ln_g", "conv_ln_b", "conv_norm",
                                        "ret_norm", "c_2", "c_ctx_2", "conv_w_2", "gm_bs_2"))),
        "conv_w_in": v["conv_w_in"][0], "conv_w_out": v["conv_w_out"][0],
        "ret_w_in": v["ret_w_in"][0], "ret_w_out": v["ret_w_out"][0],
        "gm_wsT": _np.ascontiguousarray(v["gm_ws_2"].transpose(0, 3, 1, 2)),
        "w_router": _np.ascontiguousarray(_np.concatenate([v["w_rg_2"], v["w_re_2"]], 2)),
        "b_router": _np.ascontiguousarray(_np.concatenate([v["b_rg_2"], v["b_re_2"]], 1)),
    }
    for k in ("w_ada", "b_ada", "w_in", "attn_sink", "w_out", "ln1_g", "ln1_b", "w1", "w3", "w2",
              "ln2_g", "ln2_b"):
        arrays[k] = v[k + "_2"]
    nc = _bacc.Bacc("TRN2", target_bir_lowering=False, num_devices=1)
    args = {k: nc.dram_tensor(f"in_{k}", x.shape, _mybir.dt.from_np(x.dtype), kind="ExternalInput").ap()
            for k, x in arrays.items()}
    out = nc.dram_tensor("out_x", (S, D), _mybir.dt.float32, kind="ExternalOutput").ap()
    build(nc, args, out)
    r = _run(nc, [{f"in_{k}": x for k, x in arrays.items()}], core_ids=[0])
    return r.results[0]["out_x"].reshape(1, S, D)
```
